# Optimizing a Trainium2 kernel written in Bass

```python
import jax, jax.numpy as jnp
from jax import lax
import numpy as np

D_MODEL = 1024
BATCH = 1
SEQ = 512
DEPTH = 2

N_MIXERS = 2
N_LAYERS_A = (DEPTH + N_MIXERS - 1) // N_MIXERS
N_LAYERS_B = DEPTH // N_MIXERS
D_FF = 2816
FFN_RESIDUAL_SCALE = 0.5
N_SUBLAYER_NORMS = 6
SGU_DIM = 2 * D_MODEL
SGU_GROUPS = 8
SGU_GROUP_DIM = SGU_DIM // SGU_GROUPS
CHUNK = 128
CONV_DIM = D_MODEL
CONV_WIDTH = 31
EPS = 1e-6

kernel_name = "hybrid_sgu_conformer_conv_macaron"

def rms_norm(x, g):
    xf = x.astype(jnp.float32)
    y = xf * lax.rsqrt(jnp.mean(xf * xf, axis=-1, keepdims=True) + EPS)
    return (y * g.astype(jnp.float32)).astype(x.dtype)

def layer_norm(x, g, b):
    xf = x.astype(jnp.float32)
    mu = jnp.mean(xf, axis=-1, keepdims=True)
    xc = xf - mu
    var = jnp.mean(xc * xc, axis=-1, keepdims=True)
    y = xc * lax.rsqrt(var + EPS) * g.astype(jnp.float32) + b.astype(jnp.float32)
    return y.astype(x.dtype)

def swiglu(h, w_gate, w_up, w_down):
    return (jax.nn.silu(h @ w_gate) * (h @ w_up)) @ w_down

def sgu_mixer(h, w_in, ln_g, ln_b, w_spatial, b_spatial, w_out):
    bsz, seq, _ = h.shape
    z = jax.nn.gelu(h @ w_in)
    u, v = jnp.split(z, 2, axis=-1)
    v = layer_norm(v, ln_g, ln_b)
    vc = v.reshape(bsz, seq // CHUNK, CHUNK, SGU_GROUPS, SGU_GROUP_DIM)
    causal = jnp.tril(jnp.ones((CHUNK, CHUNK), dtype=bool))
    ws = jnp.where(causal[None], w_spatial, 0)
    mixed = jnp.einsum('gts,bcsgd->bctgd', ws, vc)
    mixed = mixed + b_spatial.T[None, None, :, :, None]
    gated = u * mixed.reshape(bsz, seq, SGU_DIM)
    return gated @ w_out

def conv_mixer(h, w_pw1, w_dw, b_dw, ln_g, ln_b, w_pw2):
    a, gate = jnp.split(h @ w_pw1, 2, axis=-1)
    y = a * jax.nn.sigmoid(gate)
    y = lax.conv_general_dilated(
        y, w_dw[:, None, :].astype(y.dtype),
        window_strides=(1,),
        padding=[(CONV_WIDTH - 1, 0)],
        dimension_numbers=('NWC', 'WIO', 'NWC'),
        feature_group_count=CONV_DIM) + b_dw
    y = jax.nn.silu(layer_norm(y, ln_g, ln_b))
    return y @ w_pw2

def setup_inputs(seed: int = 0) -> dict:
    key = jax.random.key(seed)
    ks = jax.random.split(key, 18)
    f32 = jnp.float32
    nrm = lambda k, shape, scale: (jax.random.normal(k, shape, f32) * scale).astype(f32)
    x = jax.random.normal(ks[0], (BATCH, SEQ, D_MODEL), f32)
    norm_g = 1.0 + nrm(ks[1], (DEPTH, N_SUBLAYER_NORMS, D_MODEL), 0.05)
    ff_w_gate = nrm(ks[2], (DEPTH, 2, D_MODEL, D_FF), D_MODEL ** -0.5)
    ff_w_up = nrm(ks[3], (DEPTH, 2, D_MODEL, D_FF), D_MODEL ** -0.5)
    ff_w_down = nrm(ks[4], (DEPTH, 2, D_FF, D_MODEL), D_FF ** -0.5)
    sgu_w_in = nrm(ks[5], (N_LAYERS_A, D_MODEL, 2 * SGU_DIM), D_MODEL ** -0.5)
    sgu_ln_g = 1.0 + nrm(ks[6], (N_LAYERS_A, SGU_DIM), 0.05)
    sgu_ln_b = nrm(ks[7], (N_LAYERS_A, SGU_DIM), 0.02)
    sgu_w_spatial = nrm(ks[8], (N_LAYERS_A, SGU_GROUPS, CHUNK, CHUNK), CHUNK ** -0.5)
    sgu_b_spatial = 1.0 + nrm(ks[9], (N_LAYERS_A, SGU_GROUPS, CHUNK), 0.1)
    sgu_w_out = nrm(ks[10], (N_LAYERS_A, SGU_DIM, D_MODEL), SGU_DIM ** -0.5)
    conv_w_pw1 = nrm(ks[11], (N_LAYERS_B, D_MODEL, 2 * CONV_DIM), D_MODEL ** -0.5)
    conv_w_dw = nrm(ks[12], (N_LAYERS_B, CONV_WIDTH, CONV_DIM), CONV_WIDTH ** -0.5)
    conv_b_dw = nrm(ks[13], (N_LAYERS_B, CONV_DIM), 0.02)
    conv_ln_g = 1.0 + nrm(ks[14], (N_LAYERS_B, CONV_DIM), 0.05)
    conv_ln_b = nrm(ks[15], (N_LAYERS_B, CONV_DIM), 0.02)
    conv_w_pw2 = nrm(ks[16], (N_LAYERS_B, CONV_DIM, D_MODEL), CONV_DIM ** -0.5)
    return {
        "x": x, "norm_g": norm_g,
        "ff_w_gate": ff_w_gate, "ff_w_up": ff_w_up, "ff_w_down": ff_w_down,
        "sgu_w_in": sgu_w_in, "sgu_ln_g": sgu_ln_g, "sgu_ln_b": sgu_ln_b,
        "sgu_w_spatial": sgu_w_spatial, "sgu_b_spatial": sgu_b_spatial, "sgu_w_out": sgu_w_out,
        "conv_w_pw1": conv_w_pw1, "conv_w_dw": conv_w_dw, "conv_b_dw": conv_b_dw,
        "conv_ln_g": conv_ln_g, "conv_ln_b": conv_ln_b, "conv_w_pw2": conv_w_pw2,
    }

def reference(x, norm_g, ff_w_gate, ff_w_up, ff_w_down,
              sgu_w_in, sgu_ln_g, sgu_ln_b, sgu_w_spatial, sgu_b_spatial, sgu_w_out,
              conv_w_pw1, conv_w_dw, conv_b_dw, conv_ln_g, conv_ln_b, conv_w_pw2):
    for i in range(DEPTH):
        g = norm_g[i]
        h = swiglu(rms_norm(x, g[0]), ff_w_gate[i, 0], ff_w_up[i, 0], ff_w_down[i, 0])
        x = x + FFN_RESIDUAL_SCALE * rms_norm(h, g[1])
        hn = rms_norm(x, g[2])
        j = i // N_MIXERS
        if i % N_MIXERS == 0:
            m = sgu_mixer(hn, sgu_w_in[j], sgu_ln_g[j], sgu_ln_b[j],
                          sgu_w_spatial[j], sgu_b_spatial[j], sgu_w_out[j])
        else:
            m = conv_mixer(hn, conv_w_pw1[j], conv_w_dw[j], conv_b_dw[j],
                           conv_ln_g[j], conv_ln_b[j], conv_w_pw2[j])
        x = x + rms_norm(m, g[3])
        h = swiglu(rms_norm(x, g[4]), ff_w_gate[i, 1], ff_w_up[i, 1], ff_w_down[i, 1])
        x = x + FFN_RESIDUAL_SCALE * rms_norm(h, g[5])
    return x


_drawn_inputs = setup_inputs


def setup_inputs(seed=0):
    import zlib

    import numpy as np

    out = dict(_drawn_inputs(seed))
    spreads = {}
    factors = {'sgu_ln_b': 6.467, 'conv_ln_b': 5.229}
    for name, (base, spread) in spreads.items():
        noise = np.random.default_rng([zlib.crc32(name.encode()), seed]).standard_normal(out[name].shape)
        drawn = base * np.exp(spread * noise) if base else spread * noise
        out[name] = __import__('jax').numpy.asarray(drawn.astype(out[name].dtype))
    for name, factor in factors.items():
        out[name] = (out[name] * factor).astype(out[name].dtype)
    return out
```

```python
from contextlib import ExitStack

import numpy as np

import concourse.bass as bass
from concourse import mybir

F32 = mybir.dt.float32
F32R = mybir.dt.float32r
ACT = mybir.ActivationFunctionType
ALU = mybir.AluOpType

P = 128
D_MODEL = 1024
T = 512
KT = D_MODEL // P
D_FF = 2816
FT = D_FF // P
FH = FT // 2
SGU_DIM = 2 * D_MODEL
ST = SGU_DIM // P
GROUPS = 8
GT = ST // GROUPS
GD = GT * P
CHUNK = 128
NC = T // CHUNK
TAPS = 31
PAD = TAPS - 1
EPS = 1e-6
N_NORMS = 12
BLOCK = 2 * KT * P
DOWN = FH * P

O_NORM = 0
O_SGU_G = O_NORM + N_NORMS * KT
O_SGU_B = O_SGU_G + ST
O_DW_B = O_SGU_B + ST
O_CLN_G = O_DW_B + KT
O_CLN_B = O_CLN_G + KT
O_DW = O_CLN_B + KT
N_PARAM = O_DW + KT * TAPS

SUBLAYERS = [("ffn", 0, 1, 0), ("sgu", 2, 3, 0), ("ffn", 4, 5, 1),
             ("ffn", 6, 7, 2), ("conv", 8, 9, 0), ("ffn", 10, 11, 3)]


class Phase:

    def __init__(self, kind, sub, steps, cols, s0, in0, act0, prod0, out0):
        self.kind, self.sub, self.steps, self.cols = kind, sub, steps, cols
        self.s0, self.in0, self.act0, self.prod0, self.out0 = s0, in0, act0, prod0, out0
        self.next_cols = 0


def plan(n_sub):
    phases, s0, in0, act0, prod0 = [], 0, 0, 0, 0
    for q, (kind, *_rest) in enumerate(SUBLAYERS[:n_sub]):
        runs = {"ffn": [("ffn_in", FT, BLOCK, 1), ("ffn_out", 2 * KT, DOWN, 0)],
                "sgu": [("v", GROUPS, BLOCK, 2), ("u", GROUPS, BLOCK, 2), ("sgu_out", KT, BLOCK, 0)],
                "conv": [("conv_in", KT, BLOCK, 1), ("conv_out", KT // 2, BLOCK, 0)]}[kind]
        for name, steps, cols, acts in runs:
            phases.append(Phase(name, q, steps, cols, s0, in0, act0, prod0, KT * q))
            s0 += steps
            if acts:
                in0 += steps
                act0 += acts * steps
        prod0 += {"ffn": FT, "sgu": ST, "conv": KT}[kind]
    for a, b in zip(phases, phases[1:]):
        a.next_cols = b.cols
    return phases


CONV_SUB = [s[0] for s in SUBLAYERS].index("conv")


def pre_norm(q):
    return 2 * q + (q > CONV_SUB)


def post_norm(q):
    return 2 * q + 1 + (q >= CONV_SUB)


LN_NORM = 2 * CONV_SUB + 1
MEAN_CHAIN = LN_NORM


def chain(n):
    return n + (n >= LN_NORM)


def build_trunk(nc, x_in, params, sgu_spatial, sgu_bias, ffn_in_w, ffn_out_w, sgu_in_w, sgu_out_w,
                conv_in_w, conv_out_w, out, n_sub=len(SUBLAYERS)):
    phases = plan(n_sub)
    n_steps = phases[-1].s0 + phases[-1].steps

    with ExitStack() as ctx:
        base = -(-nc.sbuf_base // 64) * 64
        cursor = [base]

        def region(nbytes):
            at = cursor[0]
            cursor[0] += -(-nbytes // 64) * 64
            return at

        def sb(name, shape, dt=F32, at=None):
            n = 4 * int(np.prod(shape[1:]))
            return nc.alloc_sbuf_tensor_at(name, shape, dt, offset=region(n) if at is None else at)

        def sem(name):
            return ctx.enter_context(nc.semaphore(name))

        x_fm = sb("x_fm", [P, KT, T])
        xn_hi = sb("xn_hi", [P, KT, T], F32R)
        xn_lo_at = region(4 * KT * T)
        xn_lo = sb("xn_lo", [P, KT, T], F32R, at=xn_lo_at)
        y_out = sb("y_out", [P, KT, T], at=xn_lo_at)

        mid = region(2 * 4 * FT * T)
        h_hi = sb("h_hi", [P, FT, T], F32R, at=mid)
        h_lo = sb("h_lo", [P, FT, T], F32R, at=mid + 4 * FT * T)
        gated = sb("gated", [P, GROUPS, 2, GT, T], F32R, at=mid)
        v_tok = sb("v_tok", [P, GROUPS, NC, GD], at=mid + 32768)
        vs_hi = sb("vs_hi", [P, NC, GD], F32R, at=mid + 65536)
        vs_lo = sb("vs_lo", [P, NC, GD], F32R, at=mid + 69632)
        ws_hi = sb("ws_hi", [P, GROUPS, CHUNK], F32R, at=mid + 73728)
        ws_lo = sb("ws_lo", [P, GROUPS, CHUNK], F32R, at=mid + 77824)
        ws_rowsum = sb("ws_rowsum", [P, GROUPS, CHUNK], at=mid + 81920)
        ws_bias = sb("ws_bias", [P, GROUPS, CHUNK], at=mid + 86016)
        ws_raw = sb("ws_raw", [P, GROUPS, CHUNK], at=mid)
        conv_pad = sb("conv_pad", [P, 2, PAD + T], at=mid)
        conv_y = sb("conv_y", [P, KT, T], at=mid + 8192)
        conv_hi = sb("conv_hi", [P, KT, T], F32R, at=mid + 24576)
        conv_lo = sb("conv_lo", [P, KT, T], F32R, at=mid + 40960)
        conv_odd = sb("conv_odd", [P, T], at=mid + 57344)

        w_raw = sb("w_raw", [P, 2, BLOCK])
        w_hi = sb("w_hi", [P, 2, BLOCK], F32R)
        w_lo = sb("w_lo", [P, 2, BLOCK], F32R)

        first = sb("first", [P, 2, T])
        second = sb("second", [P, 2, T])
        sq = sb("sq", [P, 2, T])
        acc = sb("acc", [P, T])
        diag = sb("diag", [P, NC, P])
        rms_inv = sb("rms_inv", [P, T])
        mixed = sq
        shift = diag
        ident = sb("ident", [P, P])
        ones = sb("ones", [P, P])
        par = sb("par", [P, N_PARAM])
        half_g = sb("half_g", [P, N_NORMS, KT])
        stat = sb("stat", [P, NC, 1])
        root = sb("root", [P, NC, 1])
        inv = sb("inv", [P, NC, 1])
        v_stats = sb("v_stats", [P, NC, GROUPS, 6])
        v_mv = sb("v_mv", [P, NC, 2])
        v_var = sb("v_var", [P, NC, 1])
        v_root = sb("v_root", [P, NC, 1])
        v_inv = sb("v_inv", [P, NC, 1])
        v_off = sb("v_off", [P, NC, 1])
        assert cursor[0] <= nc.sbuf_usable_end, cursor[0]

        bank = [ctx.enter_context(nc.psum_tensor(f"bank{i}", [P, T], F32)) for i in range(8)]
        IN_BANKS = [(0, 1), (2, 3)]
        FIRST_BANKS = [(4, 5), (2, 3)]
        OUT_BANKS = (4, 5)
        STAT, CAST = 6, 7
        MIX_BANKS = (6, 7)

        gain = par[:, O_NORM:O_NORM + N_NORMS * KT].rearrange("p (n k) -> p n k", k=KT)
        sgu_g = par[:, O_SGU_G:O_SGU_G + ST].rearrange("p (i g t) -> p i g t", g=2, t=GT)
        sgu_b = par[:, O_SGU_B:O_SGU_B + ST].rearrange("p (i g t) -> p i g t", g=2, t=GT)
        dw_b = par[:, O_DW_B:O_DW_B + KT].rearrange("p (i t) -> p i t", t=2)
        cln_g = par[:, O_CLN_G:O_CLN_G + KT]
        cln_b = par[:, O_CLN_B:O_CLN_B + KT]
        dw = par[:, O_DW:O_DW + KT * TAPS].rearrange("p (i t j) -> p i t j", t=2, j=TAPS)

        param_loaded = sem("param_loaded")
        x_loaded = [sem(f"x_loaded{i}") for i in range(2)]
        raw_loaded = [sem(f"raw_loaded{i}") for i in range(2)]
        spatial_loaded = sem("spatial_loaded")
        bias_loaded = sem("bias_loaded")
        out_stored = sem("out_stored")
        const_ready = sem("const_ready")
        half_ready = sem("half_ready")
        hi_done = sem("hi_done")
        split_done = sem("split_done")
        step_used = sem("step_used")
        proj_ready = sem("proj_ready")
        scaled = sem("scaled")
        act_done = sem("act_done")
        prod_ready = sem("prod_ready")
        prod_hi = sem("prod_hi")
        prod_lo = sem("prod_lo")
        half_step = sem("half_step")
        out_bank_free = sem("out_bank_free")
        sq_ready = sem("sq_ready")
        acc_done = sem("acc_done")
        stat_ready = sem("stat_ready")
        ms_ready = sem("ms_ready")
        root_ready = sem("root_ready")
        inv_ready = sem("inv_ready")
        diag_ready = sem("diag_ready")
        cast_ready = sem("cast_ready")
        rms_ready = sem("rms_ready")
        y_scaled = sem("y_scaled")
        x_ready = sem("x_ready")
        xhi_ready = sem("xhi_ready")
        xlo_ready = sem("xlo_ready")
        spatial_masked = sem("spatial_masked")
        ws_hi_ready = sem("ws_hi_ready")
        ws_ready = sem("ws_ready")
        rowsum_mm = sem("rowsum_mm")
        rowsum_ready = sem("rowsum_ready")
        v_turned = sem("v_turned")
        v_copied = sem("v_copied")
        v_stats_done = sem("v_stats_done")
        v_ln = sem("v_ln")
        v_rooted = sem("v_rooted")
        v_normed = sem("v_normed")
        vs_hi_ready = sem("vs_hi_ready")
        vs_ready = sem("vs_ready")
        mix_ready = sem("mix_ready")
        shift_ready = sem("shift_ready")
        mixed_ready = sem("mixed_ready")
        conv_in_ready = sem("conv_in_ready")
        tap_done = sem("tap_done")
        mean_acc = sem("mean_acc")
        centred = sem("centred")
        conv_scaled = sem("conv_scaled")

        block = ctx.enter_context(nc.Block())

        def pairs(engine, lo, hi):
            return engine.Fori(lo, hi)

        @block.sync
        def _(sp):
            for ph in phases:
                q = SUBLAYERS[ph.sub][3]
                src = {"ffn_in": lambda: ffn_in_w[q], "ffn_out": lambda: ffn_out_w[q],
                       "v": lambda: sgu_in_w[0:GROUPS], "u": lambda: sgu_in_w[GROUPS:2 * GROUPS],
                       "sgu_out": lambda: sgu_out_w, "conv_in": lambda: conv_in_w,
                       "conv_out": lambda: conv_out_w}[ph.kind]()
                src = src.rearrange("(i t) p c -> i t p c", t=2)
                start = 0
                if ph.s0 == 0:
                    for p in range(2):
                        sp.dma_start(w_raw[:, p, 0:ph.cols], src[0, p]).then_inc(raw_loaded[p], 16)
                    start = 1
                if ph.kind == "v":
                    for p in range(2):
                        sp.wait_ge(split_done, ph.s0 + p - 1)
                        sp.dma_start(w_raw[:, p, 0:ph.cols], src[0, p]).then_inc(raw_loaded[p], 16)
                    sp.wait_ge(step_used, ph.s0)
                    sp.dma_start(ws_raw[:], sgu_spatial).then_inc(spatial_loaded, 16)
                    sp.dma_start(ws_bias[:], sgu_bias.partition_broadcast(P)).then_inc(bias_loaded, 16)
                    start = 1
                with pairs(sp, start, ph.steps // 2) as i:
                    for p in range(2):
                        sp.wait_ge(split_done, ph.s0 + p - 1 + 2 * i)
                        sp.dma_start(w_raw[:, p, 0:ph.cols], src[i, p]).then_inc(raw_loaded[p], 16)
            for k in range(KT):
                sp.wait_ge(x_ready, KT * (n_sub - 1) + k + 1)
                sp.dma_start(out[:, k, :], x_fm[:, k, :]).then_inc(out_stored, 16)
            sp.wait_ge(out_stored, 16 * KT)

        @block.gpsimd
        def _(pool):
            pool.memset(ones[:], 1.0).then_inc(const_ready, 1)
            pool.memset(ident[:], 0.0).then_inc(const_ready, 1)
            pool.wait_ge(const_ready, 2)
            pool.affine_select(out=ident[:], in_=ident[:], compare_op=ALU.not_equal, fill=1.0, base=0,
                               pattern=[[-1, P]], channel_multiplier=1).then_inc(const_ready, 1)
            if n_sub > 1:
                pool.wait_ge(spatial_loaded, 16)
                pool.affine_select(out=ws_raw[:], in_=ws_raw[:], compare_op=ALU.is_ge, fill=0.0, base=0,
                                   pattern=[[0, GROUPS], [1, CHUNK]], channel_multiplier=-1).then_inc(spatial_masked, 1)
                pool.wait_ge(v_ln, 4)
                for g in range(GROUPS):
                    for c in range(NC):
                        pool.tensor_scalar(v_tok[:, g, c, :], v_tok[:, g, c, :], v_inv[:, c, :], v_off[:, c, :],
                                           ALU.mult, ALU.add).then_inc(v_normed, 1)

        @block.scalar
        def _(act):
            act.dma_start(par[:], params).then_inc(param_loaded, 16)
            for i in range(2):
                act.dma_start(x_fm[:, 4 * i:4 * i + 4, :], x_in[:, 4 * i:4 * i + 4, :]).then_inc(x_loaded[i], 16)

            def settle():
                act.wait_ge(param_loaded, 16)

            def split_hi(s_static, i, stride, p, cols):
                if not cols:
                    return
                act.wait_ge(raw_loaded[p], 16 * (s_static // 2 + 1) + 16 * (stride // 2) * i)
                if s_static >= 2 or not isinstance(i, int):
                    act.wait_ge(step_used, s_static - 1 + stride * i)
                act.activation(w_hi[:, p, 0:cols], w_raw[:, p, 0:cols], ACT.Copy).then_inc(hi_done, 1)

            def root_of(n):
                act.wait_ge(ms_ready, n + 1)
                act.activation(root[:], stat[:], ACT.Sqrt).then_inc(root_ready, 1)

            def prepare_x(q):
                n, row = pre_norm(q), SUBLAYERS[q][1]
                for k in range(KT):
                    if q == 0:
                        if k == 0:
                            act.wait_ge(param_loaded, 16)
                        if k % 4 == 0:
                            act.wait_ge(x_loaded[k // 4], 16)
                    else:
                        act.wait_ge(x_ready, KT * (q - 1) + k + 1)
                    act.activation(xn_hi[:, k, :], x_fm[:, k, :], ACT.Identity,
                                   scale=gain[:, row, k:k + 1]).then_inc(xhi_ready, 1)
                    if k >= 2:
                        act.wait_ge(acc_done, 8 * n + k)
                    act.activation(sq[:, k % 2, :], x_fm[:, k, :], ACT.Square).then_inc(sq_ready, 1)
                root_of(n)
                act.wait_ge(cast_ready, chain(n) + 1)
                act.activation(rms_inv[:], bank[CAST][:], ACT.Copy).then_inc(rms_ready, 1)

            def evacuate(d_sq, e_static, e_dyn, n, dst, src):
                act.wait_ge(acc_done, 8 * n + e_static + e_dyn)
                act.activation(sq[:, d_sq, :], src, ACT.Square).then_inc(sq_ready, 1)
                act.activation(dst, src, ACT.Copy).then_inc(out_bank_free, 1)

            h_hi_p = h_hi[:].rearrange("p (i t) n -> p i t n", t=2)
            y_p = y_out[:].rearrange("p (i t) n -> p i t n", t=2)
            act.wait_ge(const_ready, 1)
            act.activation(root[:], ones[:, 0:NC].rearrange("p (c o) -> p c o", o=1), ACT.Copy).then_inc(out_bank_free, 2)
            for p in range(2):
                split_hi(p, 0, 0, p, phases[0].cols)

            for ph in phases:
                s0, n_pairs, kind, q = ph.s0, ph.steps // 2, ph.kind, ph.sub
                if kind in ("ffn_in", "v", "conv_in"):
                    prepare_x(q)

                if kind == "ffn_in":
                    def body(i, cols):
                        for p in range(2):
                            act.wait_ge(scaled, 2 * ph.in0 + 2 * p + 1 + 4 * i)
                            act.activation(first[:, p, :], first[:, p, :], ACT.Silu).then_inc(act_done, 1)
                            split_hi(s0 + 2 + p, i, 2, p, cols)
                            act.wait_ge(prod_ready, ph.prod0 + p + 1 + 2 * i)
                            settle()
                            act.activation(h_hi_p[:, i, p, :], second[:, p, :], ACT.Copy).then_inc(prod_hi, 1)
                    with pairs(act, 0, n_pairs - 1) as i:
                        body(i, ph.cols)
                    body(n_pairs - 1, ph.next_cols)

                elif kind == "ffn_out":
                    n = post_norm(q)

                    def body(i, cols):
                        for d in range(2):
                            last = cols != ph.cols and d == 1
                            c = cols if last else ph.cols
                            split_hi(s0 + 2 * d + 2, i, 4, 0, c)
                            act.wait_ge(step_used, s0 + 2 * d + 2 + 4 * i)
                            evacuate(d, d, 2 * i, n, y_p[:, i, d, :], bank[OUT_BANKS[d]][:])
                            split_hi(s0 + 2 * d + 3, i, 4, 1, c)
                    with pairs(act, 0, n_pairs // 2 - 1) as i:
                        body(i, ph.cols)
                    body(n_pairs // 2 - 1, ph.next_cols)

                elif kind == "v":
                    vt = v_tok[:].rearrange("p (i t) c d -> p i t c d", t=2)
                    act.wait_ge(spatial_masked, 1)
                    act.activation(ws_hi[:], ws_raw[:], ACT.Copy).then_inc(ws_hi_ready, 1)

                    def copies(dst, t_static, i):
                        for j in range(2):
                            act.wait_ge(v_turned, t_static * 2 + j + 1 + 4 * i)
                            settle()
                            act.activation(dst[:, :, j * P:(j + 1) * P],
                                           bank[MIX_BANKS[j]][:].rearrange("p (c d) -> p c d", d=P),
                                           ACT.Copy).then_inc(v_copied, 1)

                    def body(i, peeled):
                        for p in range(2):
                            for j, buf in enumerate((first, second)):
                                act.wait_ge(scaled, 2 * ph.in0 + 2 * p + j + 1 + 4 * i)
                                act.activation(buf[:, p, :], buf[:, p, :], ACT.Gelu_apprx_tanh).then_inc(act_done, 1)
                            split_hi(s0 + 2 + p, i, 2, p, ph.cols)
                            if p:
                                copies(vt[:, i, 0], 0, i)
                            elif not peeled:
                                copies(vt[:, i - 1, 1], -1, i)
                    body(0, True)
                    with pairs(act, 1, n_pairs) as i:
                        body(i, False)
                    act.wait_ge(rowsum_mm, 1)
                    for j in range(2):
                        act.activation(ws_rowsum[:, 4 * j:4 * j + 4, :],
                                       bank[OUT_BANKS[j]][:].rearrange("p (g t) -> p g t", t=CHUNK),
                                       ACT.Copy).then_inc(rowsum_ready, 1)
                    copies(vt[:, n_pairs - 1, 1], 2 * n_pairs - 1, 0)
                    act.wait_ge(v_ln, 2)
                    act.activation(v_root[:], v_var[:], ACT.Sqrt).then_inc(v_rooted, 1)

                elif kind == "u":
                    vt = v_tok[:].rearrange("p (i t) c d -> p i t c d", t=2)
                    gt = gated[:].rearrange("p (i g) h t n -> p i g h t n", g=2)

                    def body(i):
                        for p in range(2):
                            if p or not isinstance(i, int):
                                act.wait_ge(mix_ready, p + 2 * i)
                            act.wait_ge(v_normed, NC * (p + 1) + 2 * NC * i)
                            settle()
                            act.activation(vs_hi[:], vt[:, i, p], ACT.Copy).then_inc(vs_hi_ready, 1)
                            for j, buf in enumerate((first, second)):
                                act.wait_ge(scaled, 2 * ph.in0 + 2 * p + j + 1 + 4 * i)
                                act.activation(buf[:, p, :], buf[:, p, :], ACT.Gelu_apprx_tanh).then_inc(act_done, 1)
                            split_hi(s0 + 2 + p, i, 2, p, ph.cols)
                            for j, buf in enumerate((first, second)):
                                act.wait_ge(prod_ready, ph.prod0 + 2 * p + j + 1 + 4 * i)
                                settle()
                                act.activation(gt[:, i, p, 0, j, :], buf[:, p, :], ACT.Copy).then_inc(prod_hi, 1)
                    body(0)
                    with pairs(act, 1, n_pairs) as i:
                        body(i)

                elif kind == "sgu_out":
                    n = post_norm(q)

                    def body(i, cols):
                        for d in range(2):
                            act.wait_ge(step_used, s0 + d + 1 + 2 * i)
                            evacuate(d, d, 2 * i, n, y_p[:, i, d, :], bank[OUT_BANKS[d]][:])
                            split_hi(s0 + 2 + d, i, 2, d, cols)
                    with pairs(act, 0, n_pairs - 1) as i:
                        body(i, ph.cols)
                    body(n_pairs - 1, ph.next_cols)

                elif kind == "conv_in":
                    def body(i):
                        for p in range(2):
                            act.wait_ge(scaled, 2 * ph.in0 + 2 * p + 2 + 4 * i)
                            act.activation(second[:, p, :], second[:, p, :], ACT.Sigmoid).then_inc(act_done, 1)
                            split_hi(s0 + 2 + p, i, 2, p, ph.cols)
                    with pairs(act, 0, n_pairs) as i:
                        body(i)
                    for k in range(KT):
                        act.wait_ge(centred, k + 1)
                        act.wait_ge(acc_done, 8 * LN_NORM + k)
                        act.activation(sq[:, k % 2, :], conv_y[:, k, :], ACT.Square).then_inc(sq_ready, 1)
                    root_of(LN_NORM)
                    for k in range(KT):
                        act.wait_ge(conv_scaled, k + 1)
                        act.activation(conv_y[:, k, :], conv_y[:, k, :], ACT.Silu, scale=cln_g[:, k:k + 1],
                                       bias=cln_b[:, k:k + 1]).then_inc(prod_ready, 1)
                        act.wait_ge(prod_ready, ph.prod0 + k + 1)
                        act.activation(conv_hi[:, k, :], conv_y[:, k, :], ACT.Copy).then_inc(prod_hi, 1)

                elif kind == "conv_out":
                    n = post_norm(q)

                    def body(i, cols):
                        for p in range(2):
                            for d in range(2):
                                if d == 0:
                                    act.wait_ge(half_step, p + 1 + 2 * i)
                                else:
                                    act.wait_ge(step_used, s0 + p + 1 + 2 * i)
                                evacuate(d, 2 * p + d, 4 * i, n,
                                         y_out[:].rearrange("p (i t) n -> p i t n", t=4)[:, i, 2 * p + d, :],
                                         bank[OUT_BANKS[d]][:])
                            split_hi(s0 + 2 + p, i, 2, p, cols)
                    body(0, ph.cols)
                    body(1, ph.next_cols)

                if kind in ("ffn_out", "sgu_out", "conv_out"):
                    root_of(post_norm(q))

        @block.vector
        def _(dve):
            def split_lo(s_static, i, stride, p, cols):
                if not cols:
                    return
                dve.wait_ge(hi_done, s_static + 1 + stride * i)
                dve.tensor_tensor(w_lo[:, p, 0:cols], w_raw[:, p, 0:cols], w_hi[:, p, 0:cols].bitcast(F32),
                                  ALU.subtract).then_inc(split_done, 1)

            def clear_acc(n):
                dve.memset(acc[:], 0.0).then_inc(acc_done, 1)

            def add_sq(n, e_static, e_dyn, slot):
                dve.wait_ge(sq_ready, 8 * n + e_static + 1 + e_dyn)
                dve.wait_ge(acc_done, 8 * n + e_static + 1 + e_dyn)
                dve.tensor_tensor(acc[:], acc[:], sq[:, slot, :], ALU.add).then_inc(acc_done, 1)

            def inverse_root(n, scale):
                dve.wait_ge(stat_ready, chain(n) + 1)
                dve.tensor_scalar(stat[:], bank[STAT][:, 0:NC].rearrange("p (c o) -> p c o", o=1), scale, EPS,
                                  ALU.mult, ALU.add).then_inc(ms_ready, 1)
                dve.wait_ge(root_ready, n + 1)
                dve.reciprocal(inv[:], root[:]).then_inc(inv_ready, 1)
                diagonal(chain(n))

            def diagonal(c):
                dve.wait_ge(inv_ready, c + 1)
                dve.tensor_tensor(diag[:], ident[:].rearrange("p (o n) -> p o n", o=1).broadcast_to([P, NC, P]),
                                  inv[:].broadcast_to([P, NC, P]), ALU.mult).then_inc(diag_ready, 1)

            def residual_and_prepare(q_done, q_next):
                row_y = SUBLAYERS[q_done][2] if q_done is not None else None
                row_x = SUBLAYERS[q_next][1] if q_next is not None else None
                if q_done is not None:
                    dve.wait_ge(cast_ready, chain(post_norm(q_done)) + 1)
                    g_y = half_g if SUBLAYERS[q_done][0] == "ffn" else gain
                if q_next is not None:
                    n = pre_norm(q_next)
                    clear_acc(n)
                for k in range(KT + 2):
                    if q_done is not None and k < KT:
                        dve.tensor_tensor(y_out[:, k, :], y_out[:, k, :], bank[CAST][:], ALU.mult).then_inc(y_scaled, 1)
                    if q_done is not None and 1 <= k <= KT:
                        j = k - 1
                        dve.wait_ge(y_scaled, KT * q_done + j + 1)
                        dve.scalar_tensor_tensor(out=x_fm[:, j, :], in0=y_out[:, j, :], scalar=g_y[:, row_y, j:j + 1],
                                                 in1=x_fm[:, j, :], op0=ALU.mult, op1=ALU.add).then_inc(x_ready, 1)
                    if q_next is not None and k >= 2:
                        j = k - 2
                        dve.wait_ge(xhi_ready, KT * q_next + j + 1)
                        dve.scalar_tensor_tensor(out=xn_lo[:, j, :], in0=x_fm[:, j, :], scalar=gain[:, row_x, j:j + 1],
                                                 in1=xn_hi[:, j, :].bitcast(F32), op0=ALU.mult,
                                                 op1=ALU.subtract).then_inc(xlo_ready, 1)
                        if j < KT - 1:
                            add_sq(n, j, 0, j % 2)
                if q_next is not None:
                    inverse_root(n, 1.0 / D_MODEL)

            def scale_banks(ph, i, p, banks, j):
                if j == 0:
                    dve.wait_ge(proj_ready, ph.in0 + p + 1 + 2 * i)
                else:
                    dve.wait_ge(step_used, ph.s0 + p + 1 + 2 * i)
                dve.tensor_tensor((first, second)[j][:, p, :], bank[banks[p][j]][:], rms_inv[:],
                                  ALU.mult).then_inc(scaled, 1)

            h_hi_p = h_hi[:].rearrange("p (i t) n -> p i t n", t=2)
            h_lo_p = h_lo[:].rearrange("p (i t) n -> p i t n", t=2)
            dve.wait_ge(param_loaded, 16)
            dve.tensor_scalar(half_g[:], gain, 0.5, None, ALU.mult).then_inc(half_ready, 1)
            for p in range(2):
                split_lo(p, 0, 0, p, phases[0].cols)
            dve.wait_ge(half_ready, 1)
            for i in range(2):
                dve.wait_ge(x_loaded[i], 16)
            dve.wait_ge(const_ready, 3)
            residual_and_prepare(None, 0)

            for ph in phases:
                s0, n_pairs, kind, q = ph.s0, ph.steps // 2, ph.kind, ph.sub
                if kind in ("ffn_in", "v", "conv_in"):
                    dve.wait_ge(rms_ready, q + 1)

                if kind == "ffn_in":
                    def body(i, banks, cols):
                        for p in range(2):
                            scale_banks(ph, i, p, banks, 0)
                            scale_banks(ph, i, p, banks, 1)
                            dve.wait_ge(act_done, ph.act0 + p + 1 + 2 * i)
                            dve.wait_ge(scaled, 2 * ph.in0 + 2 * p + 2 + 4 * i)
                            dve.tensor_tensor(second[:, p, :], second[:, p, :], first[:, p, :],
                                              ALU.mult).then_inc(prod_ready, 1)
                            split_lo(s0 + 2 + p, i, 2, p, cols)
                            dve.wait_ge(prod_hi, ph.prod0 + p + 1 + 2 * i)
                            dve.tensor_tensor(h_lo_p[:, i, p, :], second[:, p, :], h_hi_p[:, i, p, :].bitcast(F32),
                                              ALU.subtract).then_inc(prod_lo, 1)
                    body(0, FIRST_BANKS, ph.cols)
                    with pairs(dve, 1, n_pairs - 1) as i:
                        body(i, IN_BANKS, ph.cols)
                    body(n_pairs - 1, IN_BANKS, ph.next_cols)

                elif kind == "ffn_out":
                    n = post_norm(q)
                    clear_acc(n)

                    def body(i, cols):
                        for d in range(2):
                            last = cols != ph.cols
                            c = cols if last and d == 1 else ph.cols
                            split_lo(s0 + 2 * d + 2, i, 4, 0, c)
                            if not (last and d == 1):
                                add_sq(n, d, 2 * i, d)
                            split_lo(s0 + 2 * d + 3, i, 4, 1, c)
                    with pairs(dve, 0, n_pairs // 2 - 1) as i:
                        body(i, ph.cols)
                    body(n_pairs // 2 - 1, ph.next_cols)

                elif kind == "v":
                    vt = v_tok[:].rearrange("p (i t) c d -> p i t c d", t=2)
                    vst = v_stats[:].rearrange("p c (i t) s -> p i t c s", t=2)
                    dve.wait_ge(ws_hi_ready, 1)
                    dve.tensor_tensor(ws_lo[:], ws_raw[:], ws_hi[:].bitcast(F32), ALU.subtract).then_inc(ws_ready, 1)

                    def stats(src, dst, t_static, i):
                        dve.wait_ge(v_copied, 2 * t_static + 2 + 4 * i)
                        for c in range(NC):
                            ins = dve.bn_stats(out=dst[:, c, :], in_=src[:, c, :])
                        ins.then_inc(v_stats_done, 1)

                    def body(i, banks, peeled):
                        for p in range(2):
                            if not peeled:
                                dve.wait_ge(v_turned, 2 * p - 2 + 4 * i)
                            scale_banks(ph, i, p, banks, 0)
                            scale_banks(ph, i, p, banks, 1)
                            split_lo(s0 + 2 + p, i, 2, p, ph.cols)
                            if p:
                                stats(vt[:, i, 0], vst[:, i, 0], 0, i)
                            elif not peeled:
                                stats(vt[:, i - 1, 1], vst[:, i - 1, 1], -1, i)
                    body(0, FIRST_BANKS, True)
                    with pairs(dve, 1, n_pairs) as i:
                        body(i, IN_BANKS, False)
                    stats(vt[:, n_pairs - 1, 1], vst[:, n_pairs - 1, 1], 2 * n_pairs - 1, 0)
                    dve.wait_ge(v_stats_done, GROUPS)
                    for c in range(NC):
                        ins = dve.bn_aggr(out=v_mv[:, c, :], in_=v_stats[:, c, :, :].rearrange("p g s -> p (g s)"))
                    ins.then_inc(v_ln, 1)
                    dve.wait_ge(v_ln, 1)
                    dve.tensor_scalar(v_var[:], v_mv[:, :, 1:2], EPS, None, ALU.add).then_inc(v_ln, 1)
                    dve.wait_ge(v_rooted, 1)
                    dve.reciprocal(v_inv[:], v_root[:]).then_inc(v_ln, 1)
                    dve.wait_ge(v_ln, 3)
                    dve.scalar_tensor_tensor(out=v_off[:], in0=v_mv[:, :, 0:1], scalar=-1.0, in1=v_inv[:],
                                             op0=ALU.mult, op1=ALU.mult).then_inc(v_ln, 1)

                elif kind == "u":
                    vt = v_tok[:].rearrange("p (i t) c d -> p i t c d", t=2)
                    gt = gated[:].rearrange("p (i g) h t n -> p i g h t n", g=2)
                    rs = ws_rowsum[:].rearrange("p (i g) t -> p i g t", g=2)
                    bs = ws_bias[:].rearrange("p (i g) t -> p i g t", g=2)
                    dve.wait_ge(rowsum_ready, 2)
                    dve.wait_ge(bias_loaded, 16)

                    def body(i):
                        for p in range(2):
                            dve.wait_ge(vs_hi_ready, p + 1 + 2 * i)
                            dve.tensor_tensor(vs_lo[:], vt[:, i, p], vs_hi[:].bitcast(F32),
                                              ALU.subtract).then_inc(vs_ready, 1)
                            for j in range(GT):
                                dve.scalar_tensor_tensor(out=shift[:, j, :], in0=rs[:, i, p, :],
                                                         scalar=sgu_b[:, i, p, j:j + 1], in1=bs[:, i, p, :],
                                                         op0=ALU.mult, op1=ALU.add).then_inc(shift_ready, 1)
                            scale_banks(ph, i, p, IN_BANKS, 0)
                            scale_banks(ph, i, p, IN_BANKS, 1)
                            split_lo(s0 + 2 + p, i, 2, p, ph.cols)
                            dve.wait_ge(mix_ready, p + 1 + 2 * i)
                            dve.wait_ge(shift_ready, 2 * p + 2 + 4 * i)
                            for j in range(GT):
                                dve.scalar_tensor_tensor(
                                    out=mixed[:, j, :].rearrange("p (c t) -> p c t", t=CHUNK),
                                    in0=bank[MIX_BANKS[j]][:].rearrange("p (c t) -> p c t", t=CHUNK),
                                    scalar=sgu_g[:, i, p, j:j + 1],
                                    in1=shift[:, j:j + 1, :].broadcast_to([P, NC, CHUNK]),
                                    op0=ALU.mult, op1=ALU.add).then_inc(mixed_ready, 1)
                            for j, buf in enumerate((first, second)):
                                dve.wait_ge(act_done, ph.act0 + 2 * p + j + 1 + 4 * i)
                                dve.wait_ge(mixed_ready, 2 * p + j + 1 + 4 * i)
                                dve.tensor_tensor(buf[:, p, :], buf[:, p, :], mixed[:, j, :],
                                                  ALU.mult).then_inc(prod_ready, 1)
                            for j, buf in enumerate((first, second)):
                                dve.wait_ge(prod_hi, ph.prod0 + 2 * p + j + 1 + 4 * i)
                                dve.tensor_tensor(gt[:, i, p, 1, j, :], buf[:, p, :], gt[:, i, p, 0, j, :].bitcast(F32),
                                                  ALU.subtract).then_inc(prod_lo, 1)
                    with pairs(dve, 0, n_pairs) as i:
                        body(i)

                elif kind == "sgu_out":
                    n = post_norm(q)
                    clear_acc(n)

                    def body(i, last):
                        for d in range(2):
                            if not (last and d == 1):
                                add_sq(n, d, 2 * i, d)
                            split_lo(s0 + 2 + d, i, 2, d, ph.next_cols if last else ph.cols)
                    with pairs(dve, 0, n_pairs - 1) as i:
                        body(i, False)
                    body(n_pairs - 1, True)

                elif kind == "conv_in":
                    cy = conv_y[:].rearrange("p (i t) n -> p i t n", t=2)
                    dve.memset(conv_pad[:, :, 0:PAD], 0.0).then_inc(mean_acc, 1)
                    dve.memset(acc[:], 0.0).then_inc(mean_acc, 1)
                    dve.wait_ge(mean_acc, 2)

                    def body(i, banks):
                        for p in range(2):
                            scale_banks(ph, i, p, banks, 0)
                            scale_banks(ph, i, p, banks, 1)
                            split_lo(s0 + 2 + p, i, 2, p, ph.cols)
                            dve.wait_ge(act_done, ph.act0 + p + 1 + 2 * i)
                            dve.tensor_tensor(conv_pad[:, p, PAD:], first[:, p, :], second[:, p, :],
                                              ALU.mult).then_inc(conv_in_ready, 1)
                            dve.wait_ge(conv_in_ready, p + 1 + 2 * i)
                            done, each = p * (TAPS + 1), 2 * (TAPS + 1)
                            for j in range(TAPS):
                                dst = conv_odd[:] if j % 2 else cy[:, i, p, :]
                                src = conv_pad[:, p, j:j + T]
                                w = dw[:, i, p, j:j + 1]
                                if j >= 2:
                                    dve.wait_ge(tap_done, done + j - 1 + each * i)
                                    ins = dve.scalar_tensor_tensor(out=dst, in0=src, scalar=w, in1=dst,
                                                                   op0=ALU.mult, op1=ALU.add)
                                elif j == 0:
                                    ins = dve.tensor_scalar(dst, src, w, dw_b[:, i, p:p + 1], ALU.mult, ALU.add)
                                else:
                                    ins = dve.tensor_scalar(dst, src, w, None, ALU.mult)
                                ins.then_inc(tap_done, 1)
                            dve.wait_ge(tap_done, done + TAPS + each * i)
                            dve.tensor_tensor(cy[:, i, p, :], cy[:, i, p, :], conv_odd[:], ALU.add).then_inc(tap_done, 1)
                            dve.wait_ge(tap_done, done + TAPS + 1 + each * i)
                            dve.tensor_tensor(acc[:], acc[:], cy[:, i, p, :], ALU.add).then_inc(mean_acc, 1)
                    body(0, FIRST_BANKS)
                    with pairs(dve, 1, n_pairs) as i:
                        body(i, IN_BANKS)
                    dve.wait_ge(stat_ready, MEAN_CHAIN + 1)
                    dve.tensor_scalar(inv[:], bank[STAT][:, 0:NC].rearrange("p (c o) -> p c o", o=1), 1.0 / D_MODEL,
                                      None, ALU.mult).then_inc(inv_ready, 1)
                    diagonal(MEAN_CHAIN)
                    clear_acc(LN_NORM)
                    dve.wait_ge(cast_ready, MEAN_CHAIN + 1)
                    for k in range(KT):
                        dve.tensor_tensor(conv_y[:, k, :], conv_y[:, k, :], bank[CAST][:],
                                          ALU.subtract).then_inc(centred, 1)
                        if k:
                            add_sq(LN_NORM, k - 1, 0, (k - 1) % 2)
                    inverse_root(LN_NORM, 1.0 / D_MODEL)
                    dve.wait_ge(cast_ready, chain(LN_NORM) + 1)
                    for k in range(KT + 2):
                        if k < KT:
                            dve.tensor_tensor(conv_y[:, k, :], conv_y[:, k, :], bank[CAST][:],
                                              ALU.mult).then_inc(conv_scaled, 1)
                        if k >= 2:
                            dve.wait_ge(prod_hi, ph.prod0 + k - 1)
                            dve.tensor_tensor(conv_lo[:, k - 2, :], conv_y[:, k - 2, :],
                                              conv_hi[:, k - 2, :].bitcast(F32), ALU.subtract).then_inc(prod_lo, 1)

                elif kind == "conv_out":
                    n = post_norm(q)
                    clear_acc(n)
                    for t in range(ph.steps):
                        for d in range(2):
                            if 2 * t + d < KT - 1:
                                add_sq(n, 2 * t + d, 0, d)
                        split_lo(s0 + 2 + t, 0, 0, t % 2, ph.cols if t + 2 < ph.steps else ph.next_cols)

                if kind in ("ffn_out", "sgu_out", "conv_out"):
                    inverse_root(post_norm(q), 1.0 / D_MODEL)
                    residual_and_prepare(q, q + 1 if q + 1 < n_sub else None)

        @block.tensor
        def _(pe):
            def product(dst, slot, col, x_h, x_l, start, stop):
                w_h, w_l = w_hi[:, slot, col:col + P], w_lo[:, slot, col:col + P]
                pe.matmul(dst, w_h, x_h, start=start, stop=False)
                pe.matmul(dst, w_h, x_l, start=False, stop=False)
                return pe.matmul(dst, w_l, x_h, start=False, stop=stop)

            def column_sums(n_chain, parts):
                for c in range(NC):
                    for j, part in enumerate(parts):
                        ins = pe.matmul(bank[STAT][:, c:c + 1], part[:, c * P:(c + 1) * P], ones[:, 0:1],
                                        start=(j == 0), stop=(j == len(parts) - 1))
                ins.then_inc(stat_ready, 1)

            def norm_sums(n):
                pe.wait_ge(acc_done, 8 * n + 8)
                pe.wait_ge(sq_ready, 8 * n + 8)
                column_sums(chain(n), (acc[:], sq[:, 1, :]))

            def broadcast(c):
                pe.wait_ge(diag_ready, c + 1)
                pe.matmul(bank[CAST][:], ones[:], diag[:].rearrange("p c n -> p (c n)"), start=True,
                          stop=True).then_inc(cast_ready, 1)

            def first_steps(ph):
                q, n = ph.sub, pre_norm(ph.sub)
                pe.wait_ge(split_done, ph.s0 + 2)
                spots = [(t, j, bank[FIRST_BANKS[t][j]][:]) for t in range(2) for j in range(2)]
                for k in range(KT):
                    pe.wait_ge(xhi_ready, KT * q + k + 1)
                    for t, j, dst in spots:
                        col = (j * KT + k) * P
                        pe.matmul(dst, w_hi[:, t, col:col + P], xn_hi[:, k, :], start=(k == 0), stop=False)
                        pe.matmul(dst, w_lo[:, t, col:col + P], xn_hi[:, k, :], start=False, stop=False)
                    if k == KT - 1:
                        norm_sums(n)
                    pe.wait_ge(xlo_ready, KT * q + k + 1)
                    for t, j, dst in spots:
                        col = (j * KT + k) * P
                        ins = pe.matmul(dst, w_hi[:, t, col:col + P], xn_lo[:, k, :], start=False, stop=(k == KT - 1))
                        if k == KT - 1:
                            ins.then_inc(step_used if j else proj_ready, 1)
                broadcast(chain(n))

            def in_step(ph, i, p):
                for j in range(2):
                    for k in range(KT):
                        ins = product(bank[IN_BANKS[p][j]][:], p, (j * KT + k) * P, xn_hi[:, k, :], xn_lo[:, k, :],
                                      k == 0, k == KT - 1)
                    ins.then_inc(step_used if j else proj_ready, 1)

            pe.wait_ge(const_ready, 3)
            for ph in phases:
                s0, n_pairs, kind, q = ph.s0, ph.steps // 2, ph.kind, ph.sub
                if kind in ("ffn_in", "v", "conv_in"):
                    first_steps(ph)

                def in_pair(i, second_pair):
                    for p in range(2):
                        pe.wait_ge(split_done, s0 + p + 1 + 2 * i)
                        if not (second_pair and p == 0):
                            pe.wait_ge(scaled, 2 * ph.in0 + 2 * p - 2 + 4 * i)
                        in_step(ph, i, p)

                if kind in ("ffn_in", "conv_in"):
                    in_pair(1, True)
                    with pairs(pe, 2, n_pairs) as i:
                        in_pair(i, False)

                if kind == "conv_in":
                    pe.wait_ge(mean_acc, 2 + KT)
                    column_sums(MEAN_CHAIN, (acc[:],))
                    broadcast(MEAN_CHAIN)
                    norm_sums(LN_NORM)
                    broadcast(chain(LN_NORM))

                if kind == "ffn_out":
                    with pairs(pe, 0, n_pairs // 2) as i:
                        for d in range(2):
                            pe.wait_ge(out_bank_free, ph.out0 + d + 1 + 2 * i)
                            for half in range(2):
                                pe.wait_ge(split_done, s0 + 2 * d + half + 1 + 4 * i)
                                pe.wait_ge(prod_lo, ph.prod0 + FH * (half + 1))
                                for kk in range(FH):
                                    k = half * FH + kk
                                    ins = product(bank[OUT_BANKS[d]][:], half, kk * P, h_hi[:, k, :], h_lo[:, k, :],
                                                  k == 0, k == FT - 1)
                                ins.then_inc(step_used, 1)

                if kind == "v":
                    def turn(i, p, t_static):
                        for j, buf in enumerate((first, second)):
                            pe.wait_ge(act_done, ph.act0 + 2 * t_static + j + 1 + 4 * i)
                            if not isinstance(i, int) or i or t_static:
                                pe.wait_ge(v_copied, 2 * t_static + j - 1 + 4 * i)
                            for c in range(NC):
                                ins = pe.transpose(bank[MIX_BANKS[j]][:, c * P:(c + 1) * P],
                                                   buf[:, p, c * P:(c + 1) * P], ident[:])
                            ins.then_inc(v_turned, 1)

                    def v_pair(i, second_pair):
                        for p in range(2):
                            pe.wait_ge(split_done, s0 + p + 1 + 2 * i)
                            if not (second_pair and p == 0):
                                pe.wait_ge(scaled, 2 * ph.in0 + 2 * p - 2 + 4 * i)
                            in_step(ph, i, p)
                            if p:
                                turn(i, 0, 0)
                            elif second_pair:
                                turn(0, 0, 0)
                                turn(0, 1, 1)
                            else:
                                turn(i, 1, -1)
                    v_pair(1, True)
                    with pairs(pe, 2, n_pairs) as i:
                        v_pair(i, False)
                    pe.wait_ge(ws_ready, 1)
                    for j in range(2):
                        ins = pe.matmul(bank[OUT_BANKS[j]][:], ones[:],
                                        ws_raw[:, 4 * j:4 * j + 4, :].rearrange("p g t -> p (g t)"), start=True, stop=True)
                    ins.then_inc(rowsum_mm, 1)
                    turn(0, 1, 2 * n_pairs - 1)

                if kind == "u":
                    wsh = ws_hi[:].rearrange("p (i g) t -> p i g t", g=2)
                    wsl = ws_lo[:].rearrange("p (i g) t -> p i g t", g=2)
                    with pairs(pe, 0, n_pairs) as i:
                        for p in range(2):
                            pe.wait_ge(split_done, s0 + p + 1 + 2 * i)
                            pe.wait_ge(scaled, 2 * ph.in0 + 2 * p - 2 + 4 * i)
                            in_step(ph, i, p)
                            pe.wait_ge(vs_ready, p + 1 + 2 * i)
                            if p:
                                pe.wait_ge(mixed_ready, 2 * p + 4 * i)
                            else:
                                pe.wait_ge(prod_ready, ph.prod0 + 4 * i)
                            for j in range(GT):
                                for c in range(NC):
                                    dst = bank[MIX_BANKS[j]][:, c * CHUNK:(c + 1) * CHUNK]
                                    v_h, v_l = vs_hi[:, c, j * P:(j + 1) * P], vs_lo[:, c, j * P:(j + 1) * P]
                                    pe.matmul(dst, v_h, wsh[:, i, p, :], start=True, stop=False)
                                    pe.matmul(dst, v_h, wsl[:, i, p, :], start=False, stop=False)
                                    ins = pe.matmul(dst, v_l, wsh[:, i, p, :], start=False, stop=True)
                            ins.then_inc(mix_ready, 1)

                if kind == "sgu_out":
                    with pairs(pe, 0, n_pairs) as i:
                        for d in range(2):
                            pe.wait_ge(out_bank_free, ph.out0 + d + 1 + 2 * i)
                            pe.wait_ge(split_done, s0 + d + 1 + 2 * i)
                            for k in range(ST):
                                if k in (0, ST - 4, ST - 2):
                                    pe.wait_ge(prod_lo, ph.prod0 + (ST - 4 if k == 0 else k + 2))
                                ins = product(bank[OUT_BANKS[d]][:], d, k * P, gated[:, k // GT, 0, k % GT, :],
                                              gated[:, k // GT, 1, k % GT, :], k == 0, k == ST - 1)
                            ins.then_inc(step_used, 1)

                if kind == "conv_out":
                    for t in range(ph.steps):
                        for d in range(2):
                            pe.wait_ge(out_bank_free, ph.out0 + 2 * t + d + 1)
                            pe.wait_ge(split_done, s0 + t + 1)
                            for k in range(KT):
                                if t == 0 and d == 0:
                                    pe.wait_ge(prod_lo, ph.prod0 + k + 1)
                                ins = product(bank[OUT_BANKS[d]][:], t % 2, (d * KT + k) * P, conv_hi[:, k, :],
                                              conv_lo[:, k, :], k == 0, k == KT - 1)
                            ins.then_inc(step_used if d else half_step, 1)

                if kind in ("ffn_out", "sgu_out", "conv_out"):
                    norm_sums(post_norm(q))
                    broadcast(chain(post_norm(q)))


def kernel(x, norm_g, ff_w_gate, ff_w_up, ff_w_down, sgu_w_in, sgu_ln_g, sgu_ln_b, sgu_w_spatial, sgu_b_spatial,
           sgu_w_out, conv_w_pw1, conv_w_dw, conv_b_dw, conv_ln_g, conv_ln_b, conv_w_pw2, _n_sub=len(SUBLAYERS)):
    import concourse.bacc as bacc
    from concourse.bass_utils import run_bass_kernel_spmd

    f = lambda a: np.asarray(a)
    feature = lambda a, tiles: f(a).reshape(tiles, P).T

    def in_blocks(parts, pairs_of_tiles):
        tiled = [f(w).reshape(KT, P, -1, P) for w in parts]
        return np.stack([np.concatenate([tiled[w][:, :, t, :].transpose(1, 0, 2).reshape(P, KT * P)
                                         for w, t in step], axis=1) for step in pairs_of_tiles])

    gate, up = f(ff_w_gate).reshape(4, D_MODEL, D_FF), f(ff_w_up).reshape(4, D_MODEL, D_FF)
    down = f(ff_w_down).reshape(4, 2, FH, P, KT, P)
    arrays = {
        "x_in": f(x).reshape(T, KT, P).transpose(2, 1, 0),
        "params": np.concatenate(
            [f(norm_g).reshape(N_NORMS, KT, P).transpose(2, 0, 1).reshape(P, N_NORMS * KT),
             feature(sgu_ln_g, ST), feature(sgu_ln_b, ST), feature(conv_b_dw, KT), feature(conv_ln_g, KT),
             feature(conv_ln_b, KT),
             f(conv_w_dw).reshape(TAPS, KT, P).transpose(2, 1, 0).reshape(P, KT * TAPS)], axis=1),
        "sgu_spatial": f(sgu_w_spatial).reshape(GROUPS, CHUNK, CHUNK).transpose(2, 0, 1),
        "sgu_bias": f(sgu_b_spatial).reshape(GROUPS, CHUNK),
        "ffn_in_w": np.stack([in_blocks((gate[q], up[q]), [((0, t), (1, t)) for t in range(FT)]) for q in range(4)]),
        "ffn_out_w": down.transpose(0, 4, 1, 3, 2, 5).reshape(4, 2 * KT, P, DOWN),
        "sgu_in_w": in_blocks((f(sgu_w_in)[0],), [((0, ST + 2 * g), (0, ST + 2 * g + 1)) for g in range(GROUPS)]
                              + [((0, 2 * g), (0, 2 * g + 1)) for g in range(GROUPS)]),
        "sgu_out_w": f(sgu_w_out)[0].reshape(ST, P, KT, P).transpose(2, 1, 0, 3).reshape(KT, P, ST * P),
        "conv_in_w": in_blocks((f(conv_w_pw1)[0],), [((0, t), (0, KT + t)) for t in range(KT)]),
        "conv_out_w": f(conv_w_pw2)[0].reshape(KT, P, KT // 2, 2, P).transpose(2, 1, 3, 0, 4).reshape(KT // 2, P, BLOCK),
    }
    nc = bacc.Bacc("TRN2", target_bir_lowering=False, num_devices=1)
    arrays = {name: np.ascontiguousarray(a) for name, a in arrays.items()}
    args = {name: nc.dram_tensor(name, a.shape, mybir.dt.from_np(a.dtype), kind="ExternalInput").ap()
            for name, a in arrays.items()}
    out = nc.dram_tensor("out", (P, KT, T), F32, kind="ExternalOutput").ap()
    build_trunk(nc, out=out, n_sub=_n_sub, **args)
    r = run_bass_kernel_spmd(nc, [arrays], core_ids=[0])
    return np.ascontiguousarray(np.asarray(r.results[0]["out"]).transpose(2, 1, 0)).reshape(1, T, D_MODEL)
```

```python
from contextlib import ExitStack

import numpy as np

import concourse.bass as bass
from concourse import mybir

F32 = mybir.dt.float32
F32R = mybir.dt.float32r
ACT = mybir.ActivationFunctionType
ALU = mybir.AluOpType

P = 128
D_MODEL = 1024
T = 512
KT = D_MODEL // P
D_FF = 2816
FT = D_FF // P
FH = FT // 2
SGU_DIM = 2 * D_MODEL
ST = SGU_DIM // P
GROUPS = 8
GT = ST // GROUPS
GD = GT * P
CHUNK = 128
NC = T // CHUNK
TAPS = 31
PAD = TAPS - 1
BROADCAST_AT = 1
X_TILES = 2
IN_FUNCTION = {"ffn": ACT.Silu, "sgu": ACT.Gelu_apprx_tanh, "conv": ACT.Sigmoid}
PE_TAPS = range(0, 5)
POOL_TAPS = range(5, 16)
DVE_TAPS = range(16, TAPS)
PRODUCTS = 4
EPS = 1e-6
N_NORMS = 12
BLOCK = 2 * KT * P
DOWN = FH * P
PIECES = 4
PIECE = BLOCK // PIECES

O_NORM = 0
O_SGU_G = O_NORM + N_NORMS * KT
O_SGU_B = O_SGU_G + ST
O_DW_B = O_SGU_B + ST
O_CLN_G = O_DW_B + KT
O_CLN_B = O_CLN_G + KT
O_DW = O_CLN_B + KT
N_PARAM = O_DW + KT * TAPS

SUBLAYERS = [("ffn", 0, 1, 0), ("sgu", 2, 3, 0), ("ffn", 4, 5, 1),
             ("ffn", 6, 7, 2), ("conv", 8, 9, 0), ("ffn", 10, 11, 3)]


class Phase:

    def __init__(self, kind, sub, steps, cols, s0, in0, act0, prod0, out0):
        self.kind, self.sub, self.steps, self.cols = kind, sub, steps, cols
        self.s0, self.in0, self.act0, self.prod0, self.out0 = s0, in0, act0, prod0, out0
        self.next_cols = 0


def plan(n_sub):
    phases, s0, in0, act0, prod0 = [], 0, 0, 0, 0
    for q, (kind, *_rest) in enumerate(SUBLAYERS[:n_sub]):
        runs = {"ffn": [("ffn_in", FT, BLOCK, 1), ("ffn_out", 2 * KT, DOWN, 0)],
                "sgu": [("v", GROUPS, BLOCK, 2), ("u", GROUPS, BLOCK, 2), ("sgu_out", KT, BLOCK, 0)],
                "conv": [("conv_in", KT, BLOCK, 1), ("conv_out", KT // 2, BLOCK, 0)]}[kind]
        for name, steps, cols, acts in runs:
            phases.append(Phase(name, q, steps, cols, s0, in0, act0, prod0, KT * q))
            s0 += steps
            if acts:
                in0 += steps
                act0 += acts * steps
        prod0 += {"ffn": FT, "sgu": ST, "conv": KT}[kind]
    for a, b in zip(phases, phases[1:]):
        a.next_cols = b.cols
    return phases


CONV_SUB = [s[0] for s in SUBLAYERS].index("conv")


def pre_norm(q):
    return 2 * q + (q > CONV_SUB)


def post_norm(q):
    return 2 * q + 1 + (q >= CONV_SUB)


LN_NORM = 2 * CONV_SUB + 1
MEAN_CHAIN = LN_NORM


def chain(n):
    return n + (n >= LN_NORM)


def build_trunk(nc, x_in, params, sgu_spatial, sgu_bias, ffn_in_w, ffn_out_w, sgu_in_w, sgu_out_w,
                conv_in_w, conv_out_w, out, n_sub=len(SUBLAYERS)):
    phases = plan(n_sub)
    n_steps = phases[-1].s0 + phases[-1].steps

    with ExitStack() as ctx:
        base = -(-nc.sbuf_base // 64) * 64
        cursor = [base]

        def region(nbytes):
            at = cursor[0]
            cursor[0] += -(-nbytes // 64) * 64
            return at

        def sb(name, shape, dt=F32, at=None):
            n = 4 * int(np.prod(shape[1:]))
            return nc.alloc_sbuf_tensor_at(name, shape, dt, offset=region(n) if at is None else at)

        def sem(name):
            return ctx.enter_context(nc.semaphore(name))

        x_fm = sb("x_fm", [P, KT, T])
        xn_hi = sb("xn_hi", [P, KT, T], F32R)
        xn_lo_at = region(4 * KT * T)
        xn_lo = sb("xn_lo", [P, KT, T], F32R, at=xn_lo_at)
        y_out = sb("y_out", [P, KT, T], at=xn_lo_at)

        mid = region(2 * 4 * FT * T)
        h_hi = sb("h_hi", [P, FT, T], F32R, at=mid)
        h_lo = sb("h_lo", [P, FT, T], F32R, at=mid + 4 * FT * T)
        gated = sb("gated", [P, GROUPS, 2, GT, T], F32R, at=mid)
        v_tok = sb("v_tok", [P, GROUPS, NC, GD], at=mid + 32768)
        vs_hi = sb("vs_hi", [P, NC, GD], F32R, at=mid + 65536)
        vs_lo = sb("vs_lo", [P, NC, GD], F32R, at=mid + 69632)
        ws_hi = sb("ws_hi", [P, GROUPS, CHUNK], F32R, at=mid + 73728)
        ws_lo = sb("ws_lo", [P, GROUPS, CHUNK], F32R, at=mid + 77824)
        ws_rowsum = sb("ws_rowsum", [P, GROUPS, CHUNK], at=mid + 81920)
        ws_bias = sb("ws_bias", [P, GROUPS, CHUNK], at=mid + 86016)
        ws_raw = sb("ws_raw", [P, GROUPS, CHUNK], at=mid)
        conv_pad = sb("conv_pad", [P, 2, PAD + T], at=mid)
        conv_y = sb("conv_y", [P, KT, T], at=mid + 8192)
        conv_hi = sb("conv_hi", [P, KT, T], F32R, at=mid + 24576)
        conv_lo = sb("conv_lo", [P, KT, T], F32R, at=mid + 40960)
        pool_acc = sb("pool_acc", [P, 2, T], at=mid + 57344)
        tap_product = sb("tap_product", [P, PRODUCTS, T], at=mid + 61440)
        tap_diag = sb("tap_diag", [P, 2, len(PE_TAPS), P], at=mid + 69632)

        w_raw = sb("w_raw", [P, 2, BLOCK])
        w_hi = sb("w_hi", [P, 2, BLOCK], F32R)
        w_lo = sb("w_lo", [P, 2, BLOCK], F32R)

        first = sb("first", [P, 2, T])
        second = sb("second", [P, 2, T])
        sq = sb("sq", [P, 2, T])
        acc = sb("acc", [P, T])
        diag = sb("diag", [P, NC, P])
        rms_inv = sb("rms_inv", [P, T])
        mixed = sq
        shift = diag
        ident = sb("ident", [P, P])
        ones = sb("ones", [P, P])
        par = sb("par", [P, N_PARAM])
        half_g = sb("half_g", [P, N_NORMS, KT])
        stat = sb("stat", [P, NC, 1])
        root = sb("root", [P, NC, 1])
        inv = sb("inv", [P, NC, 1])
        v_stats = sb("v_stats", [P, NC, GROUPS, 6])
        v_mv = sb("v_mv", [P, NC, 2])
        v_var = sb("v_var", [P, NC, 1])
        v_root = sb("v_root", [P, NC, 1])
        v_inv = sb("v_inv", [P, NC, 1])
        v_off = sb("v_off", [P, NC, 1])
        assert cursor[0] <= nc.sbuf_usable_end, cursor[0]

        bank = [ctx.enter_context(nc.psum_tensor(f"bank{i}", [P, T], F32)) for i in range(8)]
        IN_BANKS = [(0, 1), (2, 3)]
        FIRST_BANKS = [(4, 5), (2, 3)]
        OUT_BANKS = (4, 5)
        STAT, CAST = 6, 7
        MIX_BANKS = (6, 7)
        EVEN, ODD = 6, 7
        TAP_BANKS = (4, 5)

        gain = par[:, O_NORM:O_NORM + N_NORMS * KT].rearrange("p (n k) -> p n k", k=KT)
        sgu_g = par[:, O_SGU_G:O_SGU_G + ST].rearrange("p (i g t) -> p i g t", g=2, t=GT)
        sgu_b = par[:, O_SGU_B:O_SGU_B + ST].rearrange("p (i g t) -> p i g t", g=2, t=GT)
        dw_b = par[:, O_DW_B:O_DW_B + KT].rearrange("p (i t) -> p i t", t=2)
        cln_g = par[:, O_CLN_G:O_CLN_G + KT]
        cln_b = par[:, O_CLN_B:O_CLN_B + KT]
        dw = par[:, O_DW:O_DW + KT * TAPS].rearrange("p (i t j) -> p i t j", t=2, j=TAPS)

        param_loaded = sem("param_loaded")
        x_loaded = [sem(f"x_loaded{i}") for i in range(KT // X_TILES)]
        raw_loaded = [sem(f"raw_loaded{i}") for i in range(2)]
        spatial_loaded = sem("spatial_loaded")
        bias_loaded = sem("bias_loaded")
        out_stored = sem("out_stored")
        const_ready = sem("const_ready")
        half_ready = sem("half_ready")
        hi_done = sem("hi_done")
        split_done = sem("split_done")
        hi_piece = sem("hi_piece")
        lo_piece = sem("lo_piece")
        cols_used = sem("cols_used")
        step_used = sem("step_used")
        proj_ready = sem("proj_ready")
        scaled = sem("scaled")
        act_done = sem("act_done")
        prod_ready = sem("prod_ready")
        prod_hi = sem("prod_hi")
        prod_lo = sem("prod_lo")
        half_step = sem("half_step")
        out_bank_free = sem("out_bank_free")
        sq_ready = sem("sq_ready")
        acc_done = sem("acc_done")
        stat_ready = sem("stat_ready")
        ms_ready = sem("ms_ready")
        root_ready = sem("root_ready")
        inv_ready = sem("inv_ready")
        diag_ready = sem("diag_ready")
        cast_ready = sem("cast_ready")
        rms_ready = sem("rms_ready")
        y_scaled = sem("y_scaled")
        x_ready = sem("x_ready")
        xhi_ready = sem("xhi_ready")
        xlo_ready = sem("xlo_ready")
        spatial_masked = sem("spatial_masked")
        ws_hi_ready = sem("ws_hi_ready")
        ws_ready = sem("ws_ready")
        rowsum_mm = sem("rowsum_mm")
        rowsum_ready = sem("rowsum_ready")
        v_turned = sem("v_turned")
        v_copied = sem("v_copied")
        v_stats_done = sem("v_stats_done")
        v_ln = sem("v_ln")
        v_rooted = sem("v_rooted")
        v_normed = sem("v_normed")
        vs_hi_ready = sem("vs_hi_ready")
        vs_ready = sem("vs_ready")
        mix_ready = sem("mix_ready")
        shift_ready = sem("shift_ready")
        mixed_ready = sem("mixed_ready")
        conv_in_ready = sem("conv_in_ready")
        pad_zeroed = sem("pad_zeroed")
        diag_built = sem("diag_built")
        pe_taps = sem("pe_taps")
        product_ready = sem("product_ready")
        pool_sum = sem("pool_sum")
        tap_done = sem("tap_done")
        conv_part = sem("conv_part")
        mean_acc = sem("mean_acc")
        centred = sem("centred")
        conv_scaled = sem("conv_scaled")

        block = ctx.enter_context(nc.Block())

        def pairs(engine, lo, hi):
            return engine.Fori(lo, hi)

        @block.sync
        def _(sp):
            for ph in phases:
                q = SUBLAYERS[ph.sub][3]
                src = {"ffn_in": lambda: ffn_in_w[q], "ffn_out": lambda: ffn_out_w[q],
                       "v": lambda: sgu_in_w[0:GROUPS], "u": lambda: sgu_in_w[GROUPS:2 * GROUPS],
                       "sgu_out": lambda: sgu_out_w, "conv_in": lambda: conv_in_w,
                       "conv_out": lambda: conv_out_w}[ph.kind]()
                src = src.rearrange("(i t) p c -> i t p c", t=2)
                start = 0
                if ph.s0 == 0:
                    for p in range(2):
                        sp.dma_start(w_raw[:, p, 0:ph.cols], src[0, p]).then_inc(raw_loaded[p], 16)
                    start = 1
                if ph.kind == "v":
                    for p in range(2):
                        sp.wait_ge(split_done, ph.s0 + p - 1)
                        sp.dma_start(w_raw[:, p, 0:ph.cols], src[0, p]).then_inc(raw_loaded[p], 16)
                    sp.wait_ge(step_used, ph.s0)
                    sp.dma_start(ws_raw[:], sgu_spatial).then_inc(spatial_loaded, 16)
                    sp.dma_start(ws_bias[:], sgu_bias.partition_broadcast(P)).then_inc(bias_loaded, 16)
                    start = 1
                with pairs(sp, start, ph.steps // 2) as i:
                    for p in range(2):
                        sp.wait_ge(split_done, ph.s0 + p - 1 + 2 * i)
                        sp.dma_start(w_raw[:, p, 0:ph.cols], src[i, p]).then_inc(raw_loaded[p], 16)
            for k in range(KT):
                sp.wait_ge(x_ready, KT * (n_sub - 1) + k + 1)
                sp.dma_start(out[:, k, :], x_fm[:, k, :]).then_inc(out_stored, 16)
            sp.wait_ge(out_stored, 16 * KT)

        @block.gpsimd
        def _(pool):
            pool.memset(ones[:], 1.0).then_inc(const_ready, 1)
            pool.memset(ident[:], 0.0).then_inc(const_ready, 1)
            pool.wait_ge(const_ready, 2)
            pool.affine_select(out=ident[:], in_=ident[:], compare_op=ALU.not_equal, fill=1.0, base=0,
                               pattern=[[-1, P]], channel_multiplier=1).then_inc(const_ready, 1)
            if n_sub > 1:
                pool.wait_ge(spatial_loaded, 16)
                pool.affine_select(out=ws_raw[:], in_=ws_raw[:], compare_op=ALU.is_ge, fill=0.0, base=0,
                                   pattern=[[0, GROUPS], [1, CHUNK]], channel_multiplier=-1).then_inc(spatial_masked, 1)
                pool.wait_ge(v_ln, 4)
                for g in range(GROUPS):
                    for c in range(NC):
                        pool.tensor_scalar(v_tok[:, g, c, :], v_tok[:, g, c, :], v_inv[:, c, :], v_off[:, c, :],
                                           ALU.mult, ALU.add).then_inc(v_normed, 1)
            if n_sub > CONV_SUB:
                adds = len(POOL_TAPS) - 1

                def channel_sum(t):
                    pool.wait_ge(conv_part, 3 * (t + 1))
                    if t == 1:
                        pool.tensor_tensor(acc[:], conv_y[:, 0, :], conv_y[:, 1, :], ALU.add).then_inc(mean_acc, 1)
                    elif t > 1:
                        pool.wait_ge(mean_acc, t - 1)
                        pool.tensor_tensor(acc[:], acc[:], conv_y[:, t, :], ALU.add).then_inc(mean_acc, 1)
                for t in range(KT):
                    for n in range(adds):
                        pool.wait_ge(product_ready, t * (adds + 1) + n + 2)
                        if t or n:
                            pool.wait_ge(pool_sum, t * adds + n)
                        pool.tensor_tensor(pool_acc[:, t % 2, :], pool_acc[:, t % 2, :],
                                           tap_product[:, (t * adds + n) % PRODUCTS, :], ALU.add).then_inc(pool_sum, 1)
                    if t:
                        channel_sum(t - 1)
                channel_sum(KT - 1)

        @block.scalar
        def _(act):
            act.dma_start(par[:], params).then_inc(param_loaded, 16)
            for i in range(KT // X_TILES):
                tiles = slice(i * X_TILES, (i + 1) * X_TILES)
                act.dma_start(x_fm[:, tiles, :], x_in[:, tiles, :]).then_inc(x_loaded[i], 16)

            def settle():
                act.wait_ge(param_loaded, 16)

            def split_hi(s_static, i, stride, p, cols):
                if not cols:
                    return
                act.wait_ge(raw_loaded[p], 16 * (s_static // 2 + 1) + 16 * (stride // 2) * i)
                if s_static >= 2 or not isinstance(i, int):
                    act.wait_ge(step_used, s_static - 1 + stride * i)
                act.activation(w_hi[:, p, 0:cols], w_raw[:, p, 0:cols], ACT.Copy).then_inc(hi_done, 1)

            def hi_of_piece(s, j):
                at = slice(j * PIECE, (j + 1) * PIECE)
                act.activation(w_hi[:, s % 2, at], w_raw[:, s % 2, at],
                               ACT.Copy).then_inc(hi_piece if j < PIECES - 1 else hi_done, 1)

            def root_of(n):
                act.wait_ge(ms_ready, n + 1)
                act.activation(root[:], stat[:], ACT.Sqrt).then_inc(root_ready, 1)

            def prepare_x(q, s0):
                n, row = pre_norm(q), SUBLAYERS[q][1]
                act.wait_ge(raw_loaded[1], 16 * (s0 // 2 + 1))
                for j in range(2):
                    hi_of_piece(s0 + 1, j)
                for k in range(KT):
                    if q == 0:
                        if k == 0:
                            act.wait_ge(param_loaded, 16)
                        if k % X_TILES == 0:
                            act.wait_ge(x_loaded[k // X_TILES], 16)
                    else:
                        act.wait_ge(x_ready, KT * (q - 1) + k + 1)
                    act.activation(xn_hi[:, k, :], x_fm[:, k, :], ACT.Identity,
                                   scale=gain[:, row, k:k + 1]).then_inc(xhi_ready, 1)
                    if k >= 2:
                        act.wait_ge(acc_done, 8 * n + k)
                    act.activation(sq[:, k % 2, :], x_fm[:, k, :], ACT.Square).then_inc(sq_ready, 1)
                    if k in (1, 3):
                        hi_of_piece(s0 + 1, 2 + k // 2)
                for j in range(PIECES - 1):
                    for m in (2, 3):
                        if j == 0:
                            act.wait_ge(raw_loaded[m % 2], 16 * (s0 // 2 + 2))
                        act.wait_ge(cols_used, (PIECES - 1) * q + j + 1)
                        hi_of_piece(s0 + m, j)
                root_of(n)
                act.preload_act_table(IN_FUNCTION[SUBLAYERS[q][0]])
                act.wait_ge(step_used, s0 + 2)
                for m in (2, 3):
                    hi_of_piece(s0 + m, PIECES - 1)
                act.wait_ge(cast_ready, chain(n) + 1)
                act.activation(rms_inv[:], bank[CAST][:], ACT.Copy).then_inc(rms_ready, 1)

            def evacuate(d_sq, e_static, e_dyn, n, dst, src):
                act.wait_ge(acc_done, 8 * n + e_static + e_dyn)
                act.activation(sq[:, d_sq, :], src, ACT.Square).then_inc(sq_ready, 1)
                act.activation(dst, src, ACT.Copy).then_inc(out_bank_free, 1)

            h_hi_p = h_hi[:].rearrange("p (i t) n -> p i t n", t=2)
            y_p = y_out[:].rearrange("p (i t) n -> p i t n", t=2)
            act.wait_ge(const_ready, 1)
            act.activation(root[:], ones[:, 0:NC].rearrange("p (c o) -> p c o", o=1), ACT.Copy).then_inc(out_bank_free, 2)
            split_hi(0, 0, 0, 0, phases[0].cols)

            for ph in phases:
                s0, n_pairs, kind, q = ph.s0, ph.steps // 2, ph.kind, ph.sub
                if kind in ("ffn_in", "v", "conv_in"):
                    prepare_x(q, s0)
                elif kind != "u":
                    act.preload_act_table(ACT.Sqrt)

                if kind == "ffn_in":
                    def body(i, cols):
                        for p in range(2):
                            act.wait_ge(scaled, 2 * ph.in0 + 2 * p + 1 + 4 * i)
                            act.activation(first[:, p, :], first[:, p, :], ACT.Silu).then_inc(act_done, 1)
                            if not isinstance(i, int) or i:
                                split_hi(s0 + 2 + p, i, 2, p, cols)
                            act.wait_ge(prod_ready, ph.prod0 + p + 1 + 2 * i)
                            settle()
                            act.activation(h_hi_p[:, i, p, :], second[:, p, :], ACT.Copy).then_inc(prod_hi, 1)
                    body(0, 0)
                    with pairs(act, 1, n_pairs - 1) as i:
                        body(i, ph.cols)
                    body(n_pairs - 1, ph.next_cols)

                elif kind == "ffn_out":
                    n = post_norm(q)

                    def body(i, cols):
                        for d in range(2):
                            last = cols != ph.cols and d == 1
                            c = cols if last else ph.cols
                            split_hi(s0 + 2 * d + 2, i, 4, 0, c)
                            act.wait_ge(step_used, s0 + 2 * d + 2 + 4 * i)
                            evacuate(d, d, 2 * i, n, y_p[:, i, d, :], bank[OUT_BANKS[d]][:])
                            if not last:
                                split_hi(s0 + 2 * d + 3, i, 4, 1, c)
                    with pairs(act, 0, n_pairs // 2 - 1) as i:
                        body(i, ph.cols)
                    body(n_pairs // 2 - 1, ph.next_cols)

                elif kind == "v":
                    vt = v_tok[:].rearrange("p (i t) c d -> p i t c d", t=2)
                    act.wait_ge(spatial_masked, 1)
                    act.activation(ws_hi[:], ws_raw[:], ACT.Copy).then_inc(ws_hi_ready, 1)

                    def copies(dst, t_static, i):
                        for j in range(2):
                            act.wait_ge(v_turned, t_static * 2 + j + 1 + 4 * i)
                            settle()
                            act.activation(dst[:, :, j * P:(j + 1) * P],
                                           bank[MIX_BANKS[j]][:].rearrange("p (c d) -> p c d", d=P),
                                           ACT.Copy).then_inc(v_copied, 1)

                    def body(i, peeled):
                        for p in range(2):
                            for j, buf in enumerate((first, second)):
                                act.wait_ge(scaled, 2 * ph.in0 + 2 * p + j + 1 + 4 * i)
                                act.activation(buf[:, p, :], buf[:, p, :], ACT.Gelu_apprx_tanh).then_inc(act_done, 1)
                            if not peeled:
                                split_hi(s0 + 2 + p, i, 2, p, ph.cols)
                            if p:
                                copies(vt[:, i, 0], 0, i)
                            elif not peeled:
                                copies(vt[:, i - 1, 1], -1, i)
                    body(0, True)
                    with pairs(act, 1, n_pairs) as i:
                        body(i, False)
                    act.wait_ge(rowsum_mm, 1)
                    for j in range(2):
                        act.activation(ws_rowsum[:, 4 * j:4 * j + 4, :],
                                       bank[OUT_BANKS[j]][:].rearrange("p (g t) -> p g t", t=CHUNK),
                                       ACT.Copy).then_inc(rowsum_ready, 1)
                    copies(vt[:, n_pairs - 1, 1], 2 * n_pairs - 1, 0)
                    act.wait_ge(v_ln, 2)
                    act.activation(v_root[:], v_var[:], ACT.Sqrt).then_inc(v_rooted, 1)

                elif kind == "u":
                    vt = v_tok[:].rearrange("p (i t) c d -> p i t c d", t=2)
                    gt = gated[:].rearrange("p (i g) h t n -> p i g h t n", g=2)

                    def body(i):
                        for p in range(2):
                            if p or not isinstance(i, int):
                                act.wait_ge(mix_ready, p + 2 * i)
                            act.wait_ge(v_normed, NC * (p + 1) + 2 * NC * i)
                            settle()
                            act.activation(vs_hi[:], vt[:, i, p], ACT.Copy).then_inc(vs_hi_ready, 1)
                            for j, buf in enumerate((first, second)):
                                act.wait_ge(scaled, 2 * ph.in0 + 2 * p + j + 1 + 4 * i)
                                act.activation(buf[:, p, :], buf[:, p, :], ACT.Gelu_apprx_tanh).then_inc(act_done, 1)
                            split_hi(s0 + 2 + p, i, 2, p, ph.cols)
                            for j, buf in enumerate((first, second)):
                                act.wait_ge(prod_ready, ph.prod0 + 2 * p + j + 1 + 4 * i)
                                settle()
                                act.activation(gt[:, i, p, 0, j, :], buf[:, p, :], ACT.Copy).then_inc(prod_hi, 1)
                    body(0)
                    with pairs(act, 1, n_pairs) as i:
                        body(i)

                elif kind == "sgu_out":
                    n = post_norm(q)

                    def body(i, last):
                        for d in range(2):
                            act.wait_ge(step_used, s0 + d + 1 + 2 * i)
                            evacuate(d, d, 2 * i, n, y_p[:, i, d, :], bank[OUT_BANKS[d]][:])
                            if not (last and d == 1):
                                split_hi(s0 + 2 + d, i, 2, d, ph.next_cols if last else ph.cols)
                    with pairs(act, 0, n_pairs - 1) as i:
                        body(i, False)
                    body(n_pairs - 1, True)

                elif kind == "conv_in":
                    adds = len(POOL_TAPS) - 1
                    assert 2 * adds % PRODUCTS == 0

                    def taps(i, p):
                        later = not isinstance(i, int)
                        if later:
                            act.wait_ge(pe_taps, p - 1 + 2 * i)
                            settle()
                        for n, j in enumerate(PE_TAPS):
                            ins = act.activation(tap_diag[:, p, n, :], ident[:], ACT.Identity, scale=dw[:, i, p, j:j + 1])
                        ins.then_inc(diag_built, 1)
                        act.wait_ge(conv_in_ready, p + 1 + 2 * i)
                        if later:
                            act.wait_ge(conv_part, 3 * (p - 1) + 6 * i)
                        settle()
                        act.activation(pool_acc[:, p, :], conv_pad[:, p, POOL_TAPS[0]:POOL_TAPS[0] + T], ACT.Identity,
                                       scale=dw[:, i, p, POOL_TAPS[0]:POOL_TAPS[0] + 1],
                                       bias=dw_b[:, i, p:p + 1]).then_inc(product_ready, 1)
                        for n, j in enumerate(POOL_TAPS[1:]):
                            if later or p * adds + n >= PRODUCTS:
                                act.wait_ge(pool_sum, p * adds + n - PRODUCTS + 1 + 2 * adds * i)
                                settle()
                            act.activation(tap_product[:, (p * adds + n) % PRODUCTS, :], conv_pad[:, p, j:j + T],
                                           ACT.Identity, scale=dw[:, i, p, j:j + 1]).then_inc(product_ready, 1)

                    def body(i):
                        for p in range(2):
                            act.wait_ge(scaled, 2 * ph.in0 + 2 * p + 2 + 4 * i)
                            act.activation(second[:, p, :], second[:, p, :], ACT.Sigmoid).then_inc(act_done, 1)
                            if not isinstance(i, int):
                                split_hi(s0 + 2 + p, i, 2, p, ph.cols)
                            taps(i, p)
                    body(0)
                    with pairs(act, 1, n_pairs) as i:
                        body(i)
                    for k in range(KT):
                        act.wait_ge(centred, k + 1)
                        act.wait_ge(acc_done, 8 * LN_NORM + k)
                        act.activation(sq[:, k % 2, :], conv_y[:, k, :], ACT.Square).then_inc(sq_ready, 1)
                    root_of(LN_NORM)
                    for k in range(KT):
                        act.wait_ge(conv_scaled, k + 1)
                        act.activation(conv_y[:, k, :], conv_y[:, k, :], ACT.Silu, scale=cln_g[:, k:k + 1],
                                       bias=cln_b[:, k:k + 1]).then_inc(prod_ready, 1)
                        act.wait_ge(prod_ready, ph.prod0 + k + 1)
                        act.activation(conv_hi[:, k, :], conv_y[:, k, :], ACT.Copy).then_inc(prod_hi, 1)

                elif kind == "conv_out":
                    n = post_norm(q)

                    def body(i, cols):
                        for p in range(2):
                            for d in range(2):
                                if d == 0:
                                    act.wait_ge(half_step, p + 1 + 2 * i)
                                else:
                                    act.wait_ge(step_used, s0 + p + 1 + 2 * i)
                                evacuate(d, 2 * p + d, 4 * i, n,
                                         y_out[:].rearrange("p (i t) n -> p i t n", t=4)[:, i, 2 * p + d, :],
                                         bank[OUT_BANKS[d]][:])
                            if not (i and p):
                                split_hi(s0 + 2 + p, i, 2, p, cols)
                    body(0, ph.cols)
                    body(1, ph.next_cols)

                if kind in ("ffn_out", "sgu_out", "conv_out"):
                    root_of(post_norm(q))

        @block.vector
        def _(dve):
            def split_lo(s_static, i, stride, p, cols):
                if not cols:
                    return
                dve.wait_ge(hi_done, s_static + 1 + stride * i)
                dve.tensor_tensor(w_lo[:, p, 0:cols], w_raw[:, p, 0:cols], w_hi[:, p, 0:cols].bitcast(F32),
                                  ALU.subtract).then_inc(split_done, 1)

            def lo_of_piece(q, s0, m, j):
                if j == PIECES - 1:
                    dve.wait_ge(hi_done, s0 + m + 1)
                else:
                    count = j + 1 if m == 1 else PIECES - 1 + 2 * j + m - 1
                    dve.wait_ge(hi_piece, 3 * (PIECES - 1) * q + count)
                at, slot = slice(j * PIECE, (j + 1) * PIECE), m % 2
                dve.tensor_tensor(w_lo[:, slot, at], w_raw[:, slot, at], w_hi[:, slot, at].bitcast(F32),
                                  ALU.subtract).then_inc(lo_piece if j < PIECES - 1 else split_done, 1)

            def clear_acc(n):
                dve.memset(acc[:], 0.0).then_inc(acc_done, 1)

            def add_sq(n, e_static, e_dyn, slot):
                dve.wait_ge(sq_ready, 8 * n + e_static + 1 + e_dyn)
                dve.wait_ge(acc_done, 8 * n + e_static + 1 + e_dyn)
                dve.tensor_tensor(acc[:], acc[:], sq[:, slot, :], ALU.add).then_inc(acc_done, 1)

            def inverse_root(n, scale):
                dve.wait_ge(stat_ready, chain(n) + 1)
                dve.tensor_scalar(stat[:], bank[STAT][:, 0:NC].rearrange("p (c o) -> p c o", o=1), scale, EPS,
                                  ALU.mult, ALU.add).then_inc(ms_ready, 1)
                dve.wait_ge(root_ready, n + 1)
                dve.reciprocal(inv[:], root[:]).then_inc(inv_ready, 1)
                diagonal(chain(n))

            def diagonal(c):
                dve.wait_ge(inv_ready, c + 1)
                dve.tensor_tensor(diag[:], ident[:].rearrange("p (o n) -> p o n", o=1).broadcast_to([P, NC, P]),
                                  inv[:].broadcast_to([P, NC, P]), ALU.mult).then_inc(diag_ready, 1)

            def residual_and_prepare(q_done, q_next, s0):
                row_y = SUBLAYERS[q_done][2] if q_done is not None else None
                row_x = SUBLAYERS[q_next][1] if q_next is not None else None
                if q_next is not None:
                    n = pre_norm(q_next)
                    clear_acc(n)
                    for j in range(2):
                        lo_of_piece(q_next, s0, 1, j)
                if q_done is not None:
                    dve.wait_ge(cast_ready, chain(post_norm(q_done)) + 1)
                    g_y = half_g if SUBLAYERS[q_done][0] == "ffn" else gain

                def normed(k):
                    dve.tensor_tensor(y_out[:, k, :], y_out[:, k, :], bank[CAST][:], ALU.mult).then_inc(y_scaled, 1)

                for k in range(KT + 1):
                    if q_done is not None and k < KT:
                        if k == 0:
                            normed(0)
                        dve.wait_ge(y_scaled, KT * q_done + k + 1)
                        dve.scalar_tensor_tensor(out=x_fm[:, k, :], in0=y_out[:, k, :], scalar=g_y[:, row_y, k:k + 1],
                                                 in1=x_fm[:, k, :], op0=ALU.mult, op1=ALU.add).then_inc(x_ready, 1)
                        if k + 1 < KT:
                            normed(k + 1)
                    if q_next is not None and k >= 1:
                        j = k - 1
                        dve.wait_ge(xhi_ready, KT * q_next + j + 1)
                        dve.scalar_tensor_tensor(out=xn_lo[:, j, :], in0=x_fm[:, j, :], scalar=gain[:, row_x, j:j + 1],
                                                 in1=xn_hi[:, j, :].bitcast(F32), op0=ALU.mult,
                                                 op1=ALU.subtract).then_inc(xlo_ready, 1)
                        if j < KT - 1:
                            add_sq(n, j, 0, j % 2)
                        if j in (1, 3):
                            lo_of_piece(q_next, s0, 1, 2 + j // 2)
                if q_next is not None:
                    for j in range(PIECES - 1):
                        for m in (2, 3):
                            lo_of_piece(q_next, s0, m, j)
                    inverse_root(n, 1.0 / D_MODEL)
                    for m in (2, 3):
                        lo_of_piece(q_next, s0, m, PIECES - 1)

            def scale_banks(ph, i, p, banks, j):
                if j == 0:
                    dve.wait_ge(proj_ready, ph.in0 + p + 1 + 2 * i)
                else:
                    dve.wait_ge(step_used, ph.s0 + p + 1 + 2 * i)
                dve.tensor_tensor((first, second)[j][:, p, :], bank[banks[p][j]][:], rms_inv[:],
                                  ALU.mult).then_inc(scaled, 1)

            h_hi_p = h_hi[:].rearrange("p (i t) n -> p i t n", t=2)
            h_lo_p = h_lo[:].rearrange("p (i t) n -> p i t n", t=2)
            dve.wait_ge(param_loaded, 16)
            dve.tensor_scalar(half_g[:], gain, 0.5, None, ALU.mult).then_inc(half_ready, 1)
            split_lo(0, 0, 0, 0, phases[0].cols)
            dve.wait_ge(half_ready, 1)
            dve.wait_ge(const_ready, 3)
            residual_and_prepare(None, 0, 0)

            for ph in phases:
                s0, n_pairs, kind, q = ph.s0, ph.steps // 2, ph.kind, ph.sub
                if kind in ("ffn_in", "v", "conv_in"):
                    dve.wait_ge(rms_ready, q + 1)

                if kind == "ffn_in":
                    def body(i, banks, cols):
                        for p in range(2):
                            scale_banks(ph, i, p, banks, 0)
                            scale_banks(ph, i, p, banks, 1)
                            dve.wait_ge(act_done, ph.act0 + p + 1 + 2 * i)
                            dve.wait_ge(scaled, 2 * ph.in0 + 2 * p + 2 + 4 * i)
                            dve.tensor_tensor(second[:, p, :], second[:, p, :], first[:, p, :],
                                              ALU.mult).then_inc(prod_ready, 1)
                            if not isinstance(i, int) or i:
                                split_lo(s0 + 2 + p, i, 2, p, cols)
                            dve.wait_ge(prod_hi, ph.prod0 + p + 1 + 2 * i)
                            dve.tensor_tensor(h_lo_p[:, i, p, :], second[:, p, :], h_hi_p[:, i, p, :].bitcast(F32),
                                              ALU.subtract).then_inc(prod_lo, 1)
                    body(0, FIRST_BANKS, ph.cols)
                    with pairs(dve, 1, n_pairs - 1) as i:
                        body(i, IN_BANKS, ph.cols)
                    body(n_pairs - 1, IN_BANKS, ph.next_cols)

                elif kind == "ffn_out":
                    n = post_norm(q)
                    clear_acc(n)

                    def body(i, cols):
                        for d in range(2):
                            last = cols != ph.cols
                            c = cols if last and d == 1 else ph.cols
                            split_lo(s0 + 2 * d + 2, i, 4, 0, c)
                            if not (last and d == 1):
                                add_sq(n, d, 2 * i, d)
                            if not (last and d == 1):
                                split_lo(s0 + 2 * d + 3, i, 4, 1, c)
                    with pairs(dve, 0, n_pairs // 2 - 1) as i:
                        body(i, ph.cols)
                    body(n_pairs // 2 - 1, ph.next_cols)

                elif kind == "v":
                    vt = v_tok[:].rearrange("p (i t) c d -> p i t c d", t=2)
                    vst = v_stats[:].rearrange("p c (i t) s -> p i t c s", t=2)
                    dve.wait_ge(ws_hi_ready, 1)
                    dve.tensor_tensor(ws_lo[:], ws_raw[:], ws_hi[:].bitcast(F32), ALU.subtract).then_inc(ws_ready, 1)

                    def stats(src, dst, t_static, i):
                        dve.wait_ge(v_copied, 2 * t_static + 2 + 4 * i)
                        for c in range(NC):
                            ins = dve.bn_stats(out=dst[:, c, :], in_=src[:, c, :])
                        ins.then_inc(v_stats_done, 1)

                    def body(i, banks, peeled):
                        for p in range(2):
                            if not peeled:
                                dve.wait_ge(v_turned, 2 * p - 2 + 4 * i)
                            scale_banks(ph, i, p, banks, 0)
                            scale_banks(ph, i, p, banks, 1)
                            if not peeled:
                                split_lo(s0 + 2 + p, i, 2, p, ph.cols)
                            if p:
                                stats(vt[:, i, 0], vst[:, i, 0], 0, i)
                            elif not peeled:
                                stats(vt[:, i - 1, 1], vst[:, i - 1, 1], -1, i)
                    body(0, FIRST_BANKS, True)
                    with pairs(dve, 1, n_pairs) as i:
                        body(i, IN_BANKS, False)
                    stats(vt[:, n_pairs - 1, 1], vst[:, n_pairs - 1, 1], 2 * n_pairs - 1, 0)
                    dve.wait_ge(v_stats_done, GROUPS)
                    for c in range(NC):
                        ins = dve.bn_aggr(out=v_mv[:, c, :], in_=v_stats[:, c, :, :].rearrange("p g s -> p (g s)"))
                    ins.then_inc(v_ln, 1)
                    dve.wait_ge(v_ln, 1)
                    dve.tensor_scalar(v_var[:], v_mv[:, :, 1:2], EPS, None, ALU.add).then_inc(v_ln, 1)
                    dve.wait_ge(v_rooted, 1)
                    dve.reciprocal(v_inv[:], v_root[:]).then_inc(v_ln, 1)
                    dve.wait_ge(v_ln, 3)
                    dve.scalar_tensor_tensor(out=v_off[:], in0=v_mv[:, :, 0:1], scalar=-1.0, in1=v_inv[:],
                                             op0=ALU.mult, op1=ALU.mult).then_inc(v_ln, 1)

                elif kind == "u":
                    vt = v_tok[:].rearrange("p (i t) c d -> p i t c d", t=2)
                    gt = gated[:].rearrange("p (i g) h t n -> p i g h t n", g=2)
                    rs = ws_rowsum[:].rearrange("p (i g) t -> p i g t", g=2)
                    bs = ws_bias[:].rearrange("p (i g) t -> p i g t", g=2)
                    dve.wait_ge(rowsum_ready, 2)
                    dve.wait_ge(bias_loaded, 16)

                    def body(i):
                        for p in range(2):
                            dve.wait_ge(vs_hi_ready, p + 1 + 2 * i)
                            dve.tensor_tensor(vs_lo[:], vt[:, i, p], vs_hi[:].bitcast(F32),
                                              ALU.subtract).then_inc(vs_ready, 1)
                            for j in range(GT):
                                dve.scalar_tensor_tensor(out=shift[:, j, :], in0=rs[:, i, p, :],
                                                         scalar=sgu_b[:, i, p, j:j + 1], in1=bs[:, i, p, :],
                                                         op0=ALU.mult, op1=ALU.add).then_inc(shift_ready, 1)
                            scale_banks(ph, i, p, IN_BANKS, 0)
                            scale_banks(ph, i, p, IN_BANKS, 1)
                            split_lo(s0 + 2 + p, i, 2, p, ph.cols)
                            dve.wait_ge(mix_ready, p + 1 + 2 * i)
                            dve.wait_ge(shift_ready, 2 * p + 2 + 4 * i)
                            for j in range(GT):
                                dve.scalar_tensor_tensor(
                                    out=mixed[:, j, :].rearrange("p (c t) -> p c t", t=CHUNK),
                                    in0=bank[MIX_BANKS[j]][:].rearrange("p (c t) -> p c t", t=CHUNK),
                                    scalar=sgu_g[:, i, p, j:j + 1],
                                    in1=shift[:, j:j + 1, :].broadcast_to([P, NC, CHUNK]),
                                    op0=ALU.mult, op1=ALU.add).then_inc(mixed_ready, 1)
                            for j, buf in enumerate((first, second)):
                                dve.wait_ge(act_done, ph.act0 + 2 * p + j + 1 + 4 * i)
                                dve.wait_ge(mixed_ready, 2 * p + j + 1 + 4 * i)
                                dve.tensor_tensor(buf[:, p, :], buf[:, p, :], mixed[:, j, :],
                                                  ALU.mult).then_inc(prod_ready, 1)
                            for j, buf in enumerate((first, second)):
                                dve.wait_ge(prod_hi, ph.prod0 + 2 * p + j + 1 + 4 * i)
                                dve.tensor_tensor(gt[:, i, p, 1, j, :], buf[:, p, :], gt[:, i, p, 0, j, :].bitcast(F32),
                                                  ALU.subtract).then_inc(prod_lo, 1)
                    with pairs(dve, 0, n_pairs) as i:
                        body(i)

                elif kind == "sgu_out":
                    n = post_norm(q)
                    clear_acc(n)

                    def body(i, last):
                        for d in range(2):
                            if not (last and d == 1):
                                add_sq(n, d, 2 * i, d)
                            if not (last and d == 1):
                                split_lo(s0 + 2 + d, i, 2, d, ph.next_cols if last else ph.cols)
                    with pairs(dve, 0, n_pairs - 1) as i:
                        body(i, False)
                    body(n_pairs - 1, True)

                elif kind == "conv_in":
                    cy = conv_y[:].rearrange("p (i t) n -> p i t n", t=2)
                    dve.memset(conv_pad[:, :, 0:PAD], 0.0).then_inc(pad_zeroed, 1)
                    dve.wait_ge(pad_zeroed, 1)
                    n_dve, n_products = len(DVE_TAPS), len(POOL_TAPS)

                    def put_together(y, p, t, i):
                        dve.wait_ge(tap_done, n_dve * (t + 1) + 2 * n_dve * i)
                        dve.wait_ge(pool_sum, (n_products - 1) * (t + 1) + 2 * (n_products - 1) * i)
                        dve.tensor_tensor(y, bank[EVEN][:], pool_acc[:, p, :], ALU.add).then_inc(conv_part, 1)
                        dve.wait_ge(conv_part, 3 * t + 1 + 6 * i)
                        dve.tensor_tensor(y, bank[ODD][:], y, ALU.add).then_inc(conv_part, 1)
                        dve.wait_ge(conv_part, 3 * t + 2 + 6 * i)
                        dve.wait_ge(pe_taps, t + 1 + 2 * i)
                        dve.tensor_tensor(y, bank[TAP_BANKS[p]][:], y, ALU.add).then_inc(conv_part, 1)

                    def body(i, banks):
                        for p in range(2):
                            scale_banks(ph, i, p, banks, 0)
                            scale_banks(ph, i, p, banks, 1)
                            dve.wait_ge(act_done, ph.act0 + p + 1 + 2 * i)
                            if not isinstance(i, int):
                                dve.wait_ge(pe_taps, p - 1 + 2 * i)
                                dve.wait_ge(product_ready, n_products * (p - 1) + 2 * n_products * i)
                            dve.tensor_tensor(conv_pad[:, p, PAD:], first[:, p, :], second[:, p, :],
                                              ALU.mult).then_inc(conv_in_ready, 1)
                            if p:
                                put_together(cy[:, i, 0, :], 0, 0, i)
                            elif not isinstance(i, int):
                                put_together(cy[:, i - 1, 1, :], 1, -1, i)
                            if not isinstance(i, int):
                                split_lo(s0 + 2 + p, i, 2, p, ph.cols)
                            dve.wait_ge(conv_in_ready, p + 1 + 2 * i)
                            for n, j in enumerate(DVE_TAPS):
                                dst, src, w = bank[(EVEN, ODD)[n % 2]][:], conv_pad[:, p, j:j + T], dw[:, i, p, j:j + 1]
                                if n < 2:
                                    ins = dve.tensor_scalar(dst, src, w, None, ALU.mult)
                                else:
                                    dve.wait_ge(tap_done, n_dve * p + n - 1 + 2 * n_dve * i)
                                    ins = dve.scalar_tensor_tensor(out=dst, in0=src, scalar=w, in1=dst,
                                                                   op0=ALU.mult, op1=ALU.add)
                                ins.then_inc(tap_done, 1)
                    body(0, FIRST_BANKS)
                    with pairs(dve, 1, n_pairs) as i:
                        body(i, IN_BANKS)
                    put_together(cy[:, n_pairs - 1, 1, :], 1, ph.steps - 1, 0)
                    dve.wait_ge(stat_ready, MEAN_CHAIN + 1)
                    dve.tensor_scalar(inv[:], bank[STAT][:, 0:NC].rearrange("p (c o) -> p c o", o=1), 1.0 / D_MODEL,
                                      None, ALU.mult).then_inc(inv_ready, 1)
                    diagonal(MEAN_CHAIN)
                    clear_acc(LN_NORM)
                    dve.wait_ge(cast_ready, MEAN_CHAIN + 1)
                    for k in range(KT):
                        dve.tensor_tensor(conv_y[:, k, :], conv_y[:, k, :], bank[CAST][:],
                                          ALU.subtract).then_inc(centred, 1)
                        if k:
                            add_sq(LN_NORM, k - 1, 0, (k - 1) % 2)
                    inverse_root(LN_NORM, 1.0 / D_MODEL)
                    dve.wait_ge(cast_ready, chain(LN_NORM) + 1)
                    for k in range(KT + 2):
                        if k < KT:
                            dve.tensor_tensor(conv_y[:, k, :], conv_y[:, k, :], bank[CAST][:],
                                              ALU.mult).then_inc(conv_scaled, 1)
                        if k >= 2:
                            dve.wait_ge(prod_hi, ph.prod0 + k - 1)
                            dve.tensor_tensor(conv_lo[:, k - 2, :], conv_y[:, k - 2, :],
                                              conv_hi[:, k - 2, :].bitcast(F32), ALU.subtract).then_inc(prod_lo, 1)

                elif kind == "conv_out":
                    n = post_norm(q)
                    clear_acc(n)
                    for t in range(ph.steps):
                        for d in range(2):
                            if 2 * t + d < KT - 1:
                                add_sq(n, 2 * t + d, 0, d)
                        if t < ph.steps - 1:
                            split_lo(s0 + 2 + t, 0, 0, t % 2, ph.cols if t + 2 < ph.steps else ph.next_cols)

                if kind in ("ffn_out", "sgu_out", "conv_out"):
                    inverse_root(post_norm(q), 1.0 / D_MODEL)
                    residual_and_prepare(q, q + 1 if q + 1 < n_sub else None, s0 + ph.steps)

        @block.tensor
        def _(pe):
            def product(dst, slot, col, x_h, x_l, start, stop):
                w_h, w_l = w_hi[:, slot, col:col + P], w_lo[:, slot, col:col + P]
                pe.matmul(dst, w_h, x_h, start=start, stop=False)
                pe.matmul(dst, w_h, x_l, start=False, stop=False)
                return pe.matmul(dst, w_l, x_h, start=False, stop=stop)

            def column_sums(n_chain, parts):
                for c in range(NC):
                    for j, part in enumerate(parts):
                        ins = pe.matmul(bank[STAT][:, c:c + 1], part[:, c * P:(c + 1) * P], ones[:, 0:1],
                                        start=(j == 0), stop=(j == len(parts) - 1))
                ins.then_inc(stat_ready, 1)

            def norm_sums(n):
                pe.wait_ge(acc_done, 8 * n + 8)
                pe.wait_ge(sq_ready, 8 * n + 8)
                column_sums(chain(n), (acc[:], sq[:, 1, :]))

            def broadcast(c):
                pe.wait_ge(diag_ready, c + 1)
                pe.matmul(bank[CAST][:], ones[:], diag[:].rearrange("p c n -> p (c n)"), start=True,
                          stop=True).then_inc(cast_ready, 1)

            def first_steps(ph):
                q, n, s0 = ph.sub, pre_norm(ph.sub), ph.s0
                pe.wait_ge(split_done, s0 + 1)
                spots = [(t, j, bank[FIRST_BANKS[t][j]][:]) for t in range(2) for j in range(2)]
                for k in range(KT):
                    if k % 2 == 0 and k // 2 < PIECES - 1:
                        pe.wait_ge(lo_piece, 3 * (PIECES - 1) * q + k // 2 + 1)
                    elif k % 2 == 0:
                        pe.wait_ge(split_done, s0 + 2)
                    pe.wait_ge(xhi_ready, KT * q + k + 1)
                    for t, j, dst in spots:
                        col = (2 * k + j) * P
                        pe.matmul(dst, w_hi[:, t, col:col + P], xn_hi[:, k, :], start=(k == 0), stop=False)
                        pe.matmul(dst, w_lo[:, t, col:col + P], xn_hi[:, k, :], start=False, stop=False)
                    if k == KT - 1:
                        norm_sums(n)
                    pe.wait_ge(xlo_ready, KT * q + k + 1)
                    for t, j, dst in spots:
                        col = (2 * k + j) * P
                        ins = pe.matmul(dst, w_hi[:, t, col:col + P], xn_lo[:, k, :], start=False, stop=(k == KT - 1))
                        if k == KT - 1:
                            ins.then_inc(step_used if j else proj_ready, 1)
                    if k % 2 and k < KT - 1:
                        ins.then_inc(cols_used, 1)

            def third_step_first_tile(ph):
                for k in range(KT):
                    if k % 2 == 0 and k // 2 < PIECES - 1:
                        pe.wait_ge(lo_piece, 3 * (PIECES - 1) * ph.sub + PIECES - 1 + k + 1)
                    elif k % 2 == 0:
                        pe.wait_ge(split_done, ph.s0 + 3)
                    ins = product(bank[IN_BANKS[0][0]][:], 0, 2 * k * P, xn_hi[:, k, :], xn_lo[:, k, :],
                                  k == 0, k == KT - 1)
                    if k == BROADCAST_AT:
                        broadcast(chain(pre_norm(ph.sub)))
                ins.then_inc(proj_ready, 1)

            def in_tile(p, j):
                for k in range(KT):
                    ins = product(bank[IN_BANKS[p][j]][:], p, (2 * k + j) * P, xn_hi[:, k, :], xn_lo[:, k, :],
                                  k == 0, k == KT - 1)
                ins.then_inc(step_used if j else proj_ready, 1)

            def in_step(p):
                in_tile(p, 0)
                in_tile(p, 1)

            pe.wait_ge(const_ready, 3)
            for ph in phases:
                s0, n_pairs, kind, q = ph.s0, ph.steps // 2, ph.kind, ph.sub
                if kind in ("ffn_in", "v", "conv_in"):
                    first_steps(ph)

                def begin(i, p, second_pair):
                    if second_pair and p == 0:
                        third_step_first_tile(ph)
                        return
                    pe.wait_ge(split_done, s0 + p + 1 + 2 * i)
                    pe.wait_ge(scaled, 2 * ph.in0 + 2 * p - 2 + 4 * i)
                    in_tile(p, 0)

                def in_pair(i, second_pair):
                    for p in range(2):
                        begin(i, p, second_pair)
                        in_tile(p, 1)

                if kind == "ffn_in":
                    in_pair(1, True)
                    with pairs(pe, 2, n_pairs) as i:
                        in_pair(i, False)

                if kind == "conv_in":
                    def taps(i, p, t_static):
                        pe.wait_ge(diag_built, t_static + 1 + 2 * i)
                        pe.wait_ge(conv_in_ready, t_static + 1 + 2 * i)
                        if t_static >= 2 or not isinstance(i, int):
                            pe.wait_ge(conv_part, 3 * (t_static - 1) + 6 * i)
                        for n, j in enumerate(PE_TAPS):
                            ins = pe.matmul(bank[TAP_BANKS[p]][:], tap_diag[:, p, n, :], conv_pad[:, p, j:j + T],
                                            start=(n == 0), stop=(n == len(PE_TAPS) - 1))
                        ins.then_inc(pe_taps, 1)

                    def conv_pair(i, second_pair):
                        for p in range(2):
                            begin(i, p, second_pair)
                            if second_pair and p == 0:
                                taps(0, 0, 0)
                            elif second_pair:
                                taps(0, 0, 2)
                            else:
                                taps(i, 1 - p, p - 1)
                            in_tile(p, 1)
                            if second_pair and p == 0:
                                taps(0, 1, 1)
                    conv_pair(1, True)
                    with pairs(pe, 2, n_pairs) as i:
                        conv_pair(i, False)
                    taps(0, 1, KT - 1)
                    pe.wait_ge(mean_acc, KT - 1)
                    column_sums(MEAN_CHAIN, (acc[:],))
                    broadcast(MEAN_CHAIN)
                    norm_sums(LN_NORM)
                    broadcast(chain(LN_NORM))

                if kind == "ffn_out":
                    with pairs(pe, 0, n_pairs // 2) as i:
                        for d in range(2):
                            pe.wait_ge(out_bank_free, ph.out0 + d + 1 + 2 * i)
                            for half in range(2):
                                pe.wait_ge(split_done, s0 + 2 * d + half + 1 + 4 * i)
                                pe.wait_ge(prod_lo, ph.prod0 + FH * (half + 1))
                                for kk in range(FH):
                                    k = half * FH + kk
                                    ins = product(bank[OUT_BANKS[d]][:], half, kk * P, h_hi[:, k, :], h_lo[:, k, :],
                                                  k == 0, k == FT - 1)
                                ins.then_inc(step_used, 1)

                if kind == "v":
                    def turn(i, p, t_static):
                        for j, buf in enumerate((first, second)):
                            pe.wait_ge(act_done, ph.act0 + 2 * t_static + j + 1 + 4 * i)
                            if not isinstance(i, int) or i or t_static:
                                pe.wait_ge(v_copied, 2 * t_static + j - 1 + 4 * i)
                            for c in range(NC):
                                ins = pe.transpose(bank[MIX_BANKS[j]][:, c * P:(c + 1) * P],
                                                   buf[:, p, c * P:(c + 1) * P], ident[:])
                            ins.then_inc(v_turned, 1)

                    def v_pair(i, second_pair):
                        for p in range(2):
                            begin(i, p, second_pair)
                            in_tile(p, 1)
                            if p:
                                turn(i, 0, 0)
                            elif second_pair:
                                turn(0, 0, 0)
                                turn(0, 1, 1)
                            else:
                                turn(i, 1, -1)
                    v_pair(1, True)
                    with pairs(pe, 2, n_pairs) as i:
                        v_pair(i, False)
                    pe.wait_ge(ws_ready, 1)
                    for j in range(2):
                        ins = pe.matmul(bank[OUT_BANKS[j]][:], ones[:],
                                        ws_raw[:, 4 * j:4 * j + 4, :].rearrange("p g t -> p (g t)"), start=True, stop=True)
                    ins.then_inc(rowsum_mm, 1)
                    turn(0, 1, 2 * n_pairs - 1)

                if kind == "u":
                    wsh = ws_hi[:].rearrange("p (i g) t -> p i g t", g=2)
                    wsl = ws_lo[:].rearrange("p (i g) t -> p i g t", g=2)
                    with pairs(pe, 0, n_pairs) as i:
                        for p in range(2):
                            pe.wait_ge(split_done, s0 + p + 1 + 2 * i)
                            pe.wait_ge(scaled, 2 * ph.in0 + 2 * p - 2 + 4 * i)
                            in_step(p)
                            pe.wait_ge(vs_ready, p + 1 + 2 * i)
                            if p:
                                pe.wait_ge(mixed_ready, 2 * p + 4 * i)
                            else:
                                pe.wait_ge(prod_ready, ph.prod0 + 4 * i)
                            for j in range(GT):
                                for c in range(NC):
                                    dst = bank[MIX_BANKS[j]][:, c * CHUNK:(c + 1) * CHUNK]
                                    v_h, v_l = vs_hi[:, c, j * P:(j + 1) * P], vs_lo[:, c, j * P:(j + 1) * P]
                                    pe.matmul(dst, v_h, wsh[:, i, p, :], start=True, stop=False)
                                    pe.matmul(dst, v_h, wsl[:, i, p, :], start=False, stop=False)
                                    ins = pe.matmul(dst, v_l, wsh[:, i, p, :], start=False, stop=True)
                            ins.then_inc(mix_ready, 1)

                if kind == "sgu_out":
                    with pairs(pe, 0, n_pairs) as i:
                        for d in range(2):
                            pe.wait_ge(out_bank_free, ph.out0 + d + 1 + 2 * i)
                            pe.wait_ge(split_done, s0 + d + 1 + 2 * i)
                            for k in range(ST):
                                if k in (0, ST - 4, ST - 2):
                                    pe.wait_ge(prod_lo, ph.prod0 + (ST - 4 if k == 0 else k + 2))
                                ins = product(bank[OUT_BANKS[d]][:], d, k * P, gated[:, k // GT, 0, k % GT, :],
                                              gated[:, k // GT, 1, k % GT, :], k == 0, k == ST - 1)
                            ins.then_inc(step_used, 1)

                if kind == "conv_out":
                    for t in range(ph.steps):
                        for d in range(2):
                            pe.wait_ge(out_bank_free, ph.out0 + 2 * t + d + 1)
                            pe.wait_ge(split_done, s0 + t + 1)
                            for k in range(KT):
                                if t == 0 and d == 0:
                                    pe.wait_ge(prod_lo, ph.prod0 + k + 1)
                                ins = product(bank[OUT_BANKS[d]][:], t % 2, (d * KT + k) * P, conv_hi[:, k, :],
                                              conv_lo[:, k, :], k == 0, k == KT - 1)
                            ins.then_inc(step_used if d else half_step, 1)

                if kind in ("ffn_out", "sgu_out", "conv_out"):
                    norm_sums(post_norm(q))
                    broadcast(chain(post_norm(q)))


def kernel(x, norm_g, ff_w_gate, ff_w_up, ff_w_down, sgu_w_in, sgu_ln_g, sgu_ln_b, sgu_w_spatial, sgu_b_spatial,
           sgu_w_out, conv_w_pw1, conv_w_dw, conv_b_dw, conv_ln_g, conv_ln_b, conv_w_pw2, _n_sub=len(SUBLAYERS)):
    import concourse.bacc as bacc
    from concourse.bass_utils import run_bass_kernel_spmd

    f = lambda a: np.asarray(a)
    feature = lambda a, tiles: f(a).reshape(tiles, P).T

    def in_blocks(parts, pairs_of_tiles):
        tiled = [f(w).reshape(KT, P, -1, P) for w in parts]
        return np.stack([np.stack([tiled[w][:, :, t, :] for w, t in step], axis=1).transpose(2, 0, 1, 3).reshape(P, BLOCK)
                         for step in pairs_of_tiles])

    gate, up = f(ff_w_gate).reshape(4, D_MODEL, D_FF), f(ff_w_up).reshape(4, D_MODEL, D_FF)
    down = f(ff_w_down).reshape(4, 2, FH, P, KT, P)
    arrays = {
        "x_in": f(x).reshape(T, KT, P).transpose(2, 1, 0),
        "params": np.concatenate(
            [f(norm_g).reshape(N_NORMS, KT, P).transpose(2, 0, 1).reshape(P, N_NORMS * KT),
             feature(sgu_ln_g, ST), feature(sgu_ln_b, ST), feature(conv_b_dw, KT), feature(conv_ln_g, KT),
             feature(conv_ln_b, KT),
             f(conv_w_dw).reshape(TAPS, KT, P).transpose(2, 1, 0).reshape(P, KT * TAPS)], axis=1),
        "sgu_spatial": f(sgu_w_spatial).reshape(GROUPS, CHUNK, CHUNK).transpose(2, 0, 1),
        "sgu_bias": f(sgu_b_spatial).reshape(GROUPS, CHUNK),
        "ffn_in_w": np.stack([in_blocks((gate[q], up[q]), [((0, t), (1, t)) for t in range(FT)]) for q in range(4)]),
        "ffn_out_w": down.transpose(0, 4, 1, 3, 2, 5).reshape(4, 2 * KT, P, DOWN),
        "sgu_in_w": in_blocks((f(sgu_w_in)[0],), [((0, ST + 2 * g), (0, ST + 2 * g + 1)) for g in range(GROUPS)]
                              + [((0, 2 * g), (0, 2 * g + 1)) for g in range(GROUPS)]),
        "sgu_out_w": f(sgu_w_out)[0].reshape(ST, P, KT, P).transpose(2, 1, 0, 3).reshape(KT, P, ST * P),
        "conv_in_w": in_blocks((f(conv_w_pw1)[0],), [((0, t), (0, KT + t)) for t in range(KT)]),
        "conv_out_w": f(conv_w_pw2)[0].reshape(KT, P, KT // 2, 2, P).transpose(2, 1, 3, 0, 4).reshape(KT // 2, P, BLOCK),
    }
    nc = bacc.Bacc("TRN2", target_bir_lowering=False, num_devices=1)
    arrays = {name: np.ascontiguousarray(a) for name, a in arrays.items()}
    args = {name: nc.dram_tensor(name, a.shape, mybir.dt.from_np(a.dtype), kind="ExternalInput").ap()
            for name, a in arrays.items()}
    out = nc.dram_tensor("out", (P, KT, T), F32, kind="ExternalOutput").ap()
    build_trunk(nc, out=out, n_sub=_n_sub, **args)
    r = run_bass_kernel_spmd(nc, [arrays], core_ids=[0])
    return np.ascontiguousarray(np.asarray(r.results[0]["out"]).transpose(2, 1, 0)).reshape(1, T, D_MODEL)
```

```python
from contextlib import ExitStack

import numpy as np

import concourse.bass as bass
from concourse import mybir

F32 = mybir.dt.float32
F32R = mybir.dt.float32r
ACT = mybir.ActivationFunctionType
ALU = mybir.AluOpType

P = 128
D_MODEL = 1024
T = 512
KT = D_MODEL // P
D_FF = 2816
FT = D_FF // P
FH = FT // 2
SGU_DIM = 2 * D_MODEL
ST = SGU_DIM // P
GROUPS = 8
GT = ST // GROUPS
GD = GT * P
CHUNK = 128
NC = T // CHUNK
TAPS = 31
PAD = TAPS - 1
X_TILES = 2
HALF = T // 2
HALVES = (slice(0, HALF), slice(HALF, T))
SUM_AT, CAST_AT = 2, 7
BROADCAST_AT = 1
IN_FUNCTION = {"ffn": ACT.Silu, "sgu": ACT.Gelu_apprx_tanh, "conv": ACT.Sigmoid}
PE_TAPS = range(0, 8)
POOL_TAPS = range(8, 18)
DVE_TAPS = range(18, TAPS)
PRODUCTS = 3
PAD_SPLIT_AFTER = 1
POOL_SUM_AFTER = 2
SPLIT_AFTER = 2
EPS = 1e-6
N_NORMS = 12
BLOCK = 2 * KT * P
DOWN = FH * P
PIECES = 4
PIECE = BLOCK // PIECES

O_NORM = 0
O_SGU_G = O_NORM + N_NORMS * KT
O_SGU_B = O_SGU_G + ST
O_DW_B = O_SGU_B + ST
O_CLN_G = O_DW_B + KT
O_CLN_B = O_CLN_G + KT
O_DW = O_CLN_B + KT
N_PARAM = O_DW + KT * TAPS

SUBLAYERS = [("ffn", 0, 1, 0), ("sgu", 2, 3, 0), ("ffn", 4, 5, 1),
             ("ffn", 6, 7, 2), ("conv", 8, 9, 0), ("ffn", 10, 11, 3)]


class Phase:

    def __init__(self, kind, sub, steps, cols, s0, in0, act0, prod0, out0):
        self.kind, self.sub, self.steps, self.cols = kind, sub, steps, cols
        self.s0, self.in0, self.act0, self.prod0, self.out0 = s0, in0, act0, prod0, out0
        self.next_cols = 0


def plan(n_sub):
    phases, s0, in0, act0, prod0 = [], 0, 0, 0, 0
    for q, (kind, *_rest) in enumerate(SUBLAYERS[:n_sub]):
        runs = {"ffn": [("ffn_in", FT, BLOCK, 1), ("ffn_out", 2 * KT, DOWN, 0)],
                "sgu": [("v", GROUPS, BLOCK, 2), ("u", GROUPS, BLOCK, 2), ("sgu_out", KT, BLOCK, 0)],
                "conv": [("conv_in", KT, BLOCK, 1), ("conv_out", KT // 2, BLOCK, 0)]}[kind]
        for name, steps, cols, acts in runs:
            phases.append(Phase(name, q, steps, cols, s0, in0, act0, prod0, KT * q))
            s0 += steps
            if acts:
                in0 += steps
                act0 += acts * steps
        prod0 += {"ffn": FT, "sgu": ST, "conv": KT}[kind]
    for a, b in zip(phases, phases[1:]):
        a.next_cols = b.cols
    return phases


CONV_SUB = [s[0] for s in SUBLAYERS].index("conv")


def pre_norm(q):
    return 2 * q


def post_norm(q):
    return 2 * q + 1


def acc_base(n):
    return (3 * KT - 1) * (n // 2) + (2 * KT - 1) * (n % 2)


def sq_base(n):
    return (3 * KT + 1) * (n // 2) + 2 * KT * (n % 2)


def trip(n, h=0):
    return 3 * (n // 2) + n % 2 + h


def build_trunk(nc, x_in, params, sgu_spatial, sgu_bias, ffn_in_w, ffn_out_w, sgu_in_w, sgu_out_w,
                conv_in_w, conv_out_w, out, n_sub=len(SUBLAYERS)):
    phases = plan(n_sub)
    n_steps = phases[-1].s0 + phases[-1].steps

    with ExitStack() as ctx:
        base = -(-nc.sbuf_base // 64) * 64
        cursor = [base]

        def region(nbytes):
            at = cursor[0]
            cursor[0] += -(-nbytes // 64) * 64
            return at

        def sb(name, shape, dt=F32, at=None):
            n = 4 * int(np.prod(shape[1:]))
            return nc.alloc_sbuf_tensor_at(name, shape, dt, offset=region(n) if at is None else at)

        def sem(name):
            return ctx.enter_context(nc.semaphore(name))

        x_fm = sb("x_fm", [P, KT, T])
        xn_hi = sb("xn_hi", [P, KT, T], F32R)
        xn_lo_at = region(4 * KT * T)
        xn_lo = sb("xn_lo", [P, KT, T], F32R, at=xn_lo_at)
        y_out = sb("y_out", [P, KT, T], at=xn_lo_at)

        mid = region(2 * 4 * FT * T)
        h_hi = sb("h_hi", [P, FT, T], F32R, at=mid)
        h_lo = sb("h_lo", [P, FT, T], F32R, at=mid + 4 * FT * T)
        gated = sb("gated", [P, GROUPS, 2, GT, T], F32R, at=mid)
        v_tok = sb("v_tok", [P, GROUPS, NC, GD], at=mid + 32768)
        vs_hi = sb("vs_hi", [P, NC, GD], F32R, at=mid + 65536)
        vs_lo = sb("vs_lo", [P, NC, GD], F32R, at=mid + 69632)
        ws_hi = sb("ws_hi", [P, GROUPS, CHUNK], F32R, at=mid + 73728)
        ws_lo = sb("ws_lo", [P, GROUPS, CHUNK], F32R, at=mid + 77824)
        ws_rowsum = sb("ws_rowsum", [P, GROUPS, CHUNK], at=mid + 81920)
        ws_bias = sb("ws_bias", [P, GROUPS, CHUNK], at=mid + 86016)
        ws_raw = sb("ws_raw", [P, GROUPS, CHUNK], at=mid)
        conv_pad = sb("conv_pad", [P, 2, PAD + T], at=mid)
        dw_hi = sb("dw_hi", [P, KT * TAPS], F32R, at=mid + 5120)
        dw_lo = sb("dw_lo", [P, KT * TAPS], at=mid + 6144)
        conv_y = sb("conv_y", [P, KT, T], at=mid + 8192)
        conv_hi = sb("conv_hi", [P, KT, T], F32R, at=mid + 24576)
        pad_hi = sb("pad_hi", [P, 2, PAD + T], F32R, at=mid + 24576)
        pad_lo = sb("pad_lo", [P, 2, PAD + T], F32R, at=mid + 32768)
        conv_lo = sb("conv_lo", [P, KT, T], F32R, at=mid + 40960)
        pool_acc = sb("pool_acc", [P, 2, T], at=mid + 57344)
        tap_product = sb("tap_product", [P, PRODUCTS, T], at=mid + 61440)
        tap_hi = sb("tap_hi", [P, 2, len(PE_TAPS), P], F32R, at=mid + 69632)
        tap_lo = sb("tap_lo", [P, 2, len(PE_TAPS), P], F32R, at=mid + 69632 + 1024 * len(PE_TAPS))
        sq_sum = sb("sq_sum", [P, T], at=mid + 86016)
        even_sum = sb("even_sum", [P, T], at=mid + 88064)
        assert 69632 + 2048 * len(PE_TAPS) <= 86016 and 88064 + 4 * T <= 2 * 4 * FT * T

        w_raw = sb("w_raw", [P, 2, BLOCK])
        w_hi = sb("w_hi", [P, 2, BLOCK], F32R)
        w_lo = sb("w_lo", [P, 2, BLOCK], F32R)

        first = sb("first", [P, 2, T])
        second = sb("second", [P, 2, T])
        sq = sb("sq", [P, 2, T])
        acc = sb("acc", [P, T])
        diag = sb("diag", [P, NC, P])
        rms_inv = sb("rms_inv", [P, T])
        mixed = sq
        shift = diag
        neg_c = diag[:].rearrange("p c n -> p (c n)")
        ident = sb("ident", [P, P])
        ones = sb("ones", [P, P])
        par = sb("par", [P, N_PARAM])
        half_g = sb("half_g", [P, N_NORMS, KT])
        eps = sb("eps", [P, 1])
        stat_part = sb("stat_part", [P, 2 * NC, 1])
        stat = sb("stat", [P, 2 * NC, 1])
        root = sb("root", [P, NC, 1])
        inv = sb("inv", [P, NC, 1])
        v_stats = sb("v_stats", [P, NC, GROUPS, 6])
        v_mv = sb("v_mv", [P, NC, 2])
        v_var = sb("v_var", [P, NC, 1])
        v_root = sb("v_root", [P, NC, 1])
        v_inv = sb("v_inv", [P, NC, 1])
        v_off = sb("v_off", [P, NC, 1])
        assert cursor[0] <= nc.sbuf_usable_end, cursor[0]

        bank = [ctx.enter_context(nc.psum_tensor(f"bank{i}", [P, T], F32)) for i in range(8)]
        IN_BANKS = [(0, 1), (2, 3)]
        FIRST_BANKS = [(4, 5), (2, 3)]
        OUT_BANKS = (4, 5)
        LAST_BANKS = (5, 0)
        CAST_HALVES = (7, 1)
        STAT, CAST = 6, 7
        MIX_BANKS = (6, 7)
        ODD = 7
        TAP_BANKS = (4, 5)
        LN_SUM, LN_CAST = 0, 1
        LN_PART, LN_STAT = 2, 3
        CONV_OUT_BANKS = (4, 5, 6, 7, 0, 1, 2)

        gain = par[:, O_NORM:O_NORM + N_NORMS * KT].rearrange("p (n k) -> p n k", k=KT)
        sgu_g = par[:, O_SGU_G:O_SGU_G + ST].rearrange("p (i g t) -> p i g t", g=2, t=GT)
        sgu_b = par[:, O_SGU_B:O_SGU_B + ST].rearrange("p (i g t) -> p i g t", g=2, t=GT)
        dw_b = par[:, O_DW_B:O_DW_B + KT].rearrange("p (i t) -> p i t", t=2)
        cln_g = par[:, O_CLN_G:O_CLN_G + KT]
        cln_b = par[:, O_CLN_B:O_CLN_B + KT]
        dw_all = par[:, O_DW:O_DW + KT * TAPS]
        dw, dwh, dwl = (a.rearrange("p (i t j) -> p i t j", t=2, j=TAPS)
                        for a in (dw_all, dw_hi[:].bitcast(F32), dw_lo[:]))

        param_loaded = sem("param_loaded")
        x_loaded = [[sem(f"x_loaded{h}{i}") for i in range(KT // X_TILES)] for h in range(2)]
        piece_loaded = [[sem(f"piece_loaded{p}{j}") for j in range(PIECES - 1)] for p in range(2)]
        first_lo = sem("first_lo")
        first_hi = sem("first_hi")
        raw_loaded = [sem(f"raw_loaded{i}") for i in range(2)]
        spatial_loaded = sem("spatial_loaded")
        bias_loaded = sem("bias_loaded")
        out_stored = sem("out_stored")
        const_ready = sem("const_ready")
        half_ready = sem("half_ready")
        hi_done = sem("hi_done")
        split_done = sem("split_done")
        hi_piece = sem("hi_piece")
        lo_piece = sem("lo_piece")
        cols_used = sem("cols_used")
        step_used = sem("step_used")
        proj_ready = sem("proj_ready")
        scaled = sem("scaled")
        act_done = sem("act_done")
        prod_ready = sem("prod_ready")
        prod_hi = sem("prod_hi")
        prod_lo = sem("prod_lo")
        last_half = sem("last_half")
        half_step = sem("half_step")
        out_bank_free = sem("out_bank_free")
        sq_ready = sem("sq_ready")
        acc_done = sem("acc_done")
        stat_part_ready = sem("stat_part_ready")
        stat_ready = sem("stat_ready")
        part_ready = sem("part_ready")
        ms_ready = sem("ms_ready")
        root_ready = sem("root_ready")
        inv_ready = sem("inv_ready")
        diag_ready = sem("diag_ready")
        cast_ready = sem("cast_ready")
        rms_ready = sem("rms_ready")
        y_scaled = sem("y_scaled")
        x_ready = sem("x_ready")
        odd_x_ready = sem("odd_x_ready")
        xhi_ready = sem("xhi_ready")
        xlo_ready = sem("xlo_ready")
        spatial_masked = sem("spatial_masked")
        ws_hi_ready = sem("ws_hi_ready")
        ws_ready = sem("ws_ready")
        rowsum_mm = sem("rowsum_mm")
        rowsum_ready = sem("rowsum_ready")
        v_turned = sem("v_turned")
        v_copied = sem("v_copied")
        v_stats_done = sem("v_stats_done")
        v_ln = sem("v_ln")
        v_rooted = sem("v_rooted")
        v_normed = sem("v_normed")
        vs_hi_ready = sem("vs_hi_ready")
        vs_ready = sem("vs_ready")
        mix_ready = sem("mix_ready")
        shift_ready = sem("shift_ready")
        mixed_ready = sem("mixed_ready")
        conv_in_ready = sem("conv_in_ready")
        pad_zeroed = sem("pad_zeroed")
        diag_built = sem("diag_built")
        pe_taps = sem("pe_taps")
        product_ready = sem("product_ready")
        pool_sum = sem("pool_sum")
        tap_done = sem("tap_done")
        conv_part = sem("conv_part")
        dw_hi_ready = sem("dw_hi_ready")
        dw_ready = sem("dw_ready")
        pad_hi_ready = sem("pad_hi_ready")
        pad_ready = sem("pad_ready")
        c_ready = sem("c_ready")
        neg_c_ready = sem("neg_c_ready")
        shifted = sem("shifted")
        conv_sq = sem("conv_sq")
        conv_sq_free = sem("conv_sq_free")
        ln_part = sem("ln_part")
        ln_part_read = sem("ln_part_read")
        ln_stat = sem("ln_stat")
        ln_sum = sem("ln_sum")
        ln_step = sem("ln_step")
        ln_root = sem("ln_root")
        ln_inv = sem("ln_inv")
        ln_diag = sem("ln_diag")
        ln_cast = sem("ln_cast")
        centred = sem("centred")
        conv_scaled = sem("conv_scaled")

        block = ctx.enter_context(nc.Block())

        def pairs(engine, lo, hi):
            return engine.Fori(lo, hi)

        def load_x(sp, h, i):
            tiles = slice(i * X_TILES, (i + 1) * X_TILES)
            sp.dma_start(x_fm[:, tiles, HALVES[h]], x_in[:, tiles, HALVES[h]]).then_inc(x_loaded[h][i], 16)

        @block.sync
        def _(sp):
            for ph in phases:
                q = SUBLAYERS[ph.sub][3]
                src = {"ffn_in": lambda: ffn_in_w[q], "ffn_out": lambda: ffn_out_w[q],
                       "v": lambda: sgu_in_w[0:GROUPS], "u": lambda: sgu_in_w[GROUPS:2 * GROUPS],
                       "sgu_out": lambda: sgu_out_w, "conv_in": lambda: conv_in_w,
                       "conv_out": lambda: conv_out_w}[ph.kind]()
                src = src.rearrange("(i t) p c -> i t p c", t=2)
                start = 0
                if ph.s0 == 0:
                    for j in range(PIECES):
                        at = slice(j * PIECE, (j + 1) * PIECE)
                        for p in range(2):
                            sp.dma_start(w_raw[:, p, at], src[0, p][:, at]).then_inc(
                                piece_loaded[p][j] if j < PIECES - 1 else raw_loaded[p], 16)
                            if p == 0:
                                load_x(sp, 0, j)
                    for j in range(PIECES):
                        load_x(sp, 1, j)
                    start = 1
                if ph.kind == "v":
                    for p in range(2):
                        sp.wait_ge(split_done, ph.s0 + p - 1)
                        sp.dma_start(w_raw[:, p, 0:ph.cols], src[0, p]).then_inc(raw_loaded[p], 16)
                    sp.wait_ge(step_used, ph.s0)
                    sp.dma_start(ws_raw[:], sgu_spatial).then_inc(spatial_loaded, 16)
                    sp.dma_start(ws_bias[:], sgu_bias.partition_broadcast(P)).then_inc(bias_loaded, 16)
                    start = 1
                with pairs(sp, start, ph.steps // 2) as i:
                    for p in range(2):
                        sp.wait_ge(split_done, ph.s0 + p - 1 + 2 * i)
                        sp.dma_start(w_raw[:, p, 0:ph.cols], src[i, p]).then_inc(raw_loaded[p], 16)
            for h, half in enumerate(HALVES):
                for k in range(0, KT, X_TILES):
                    sp.wait_ge(x_ready, 2 * KT * (n_sub - 1) + (KT * h + k) // 2 + 1)
                    sp.wait_ge(odd_x_ready, (KT * h + k) // 2 + 1)
                    sp.dma_start(out[:, k:k + X_TILES, half], x_fm[:, k:k + X_TILES, half]).then_inc(out_stored, 16)
            sp.wait_ge(out_stored, 16 * 2 * KT // X_TILES)

        @block.gpsimd
        def _(pool):
            pool.memset(eps[:], EPS).then_inc(const_ready, 1)
            pool.memset(ones[:], 1.0).then_inc(const_ready, 1)
            pool.memset(ident[:], 0.0).then_inc(const_ready, 1)
            pool.wait_ge(const_ready, 3)
            pool.affine_select(out=ident[:], in_=ident[:], compare_op=ALU.not_equal, fill=1.0, base=0,
                               pattern=[[-1, P]], channel_multiplier=1).then_inc(const_ready, 1)

            def pre_norm_sums(q):
                n = pre_norm(q)
                if q:
                    pool.wait_ge(stat_part_ready, n)
                pool.memset(acc[:], 0.0).then_inc(acc_done, 1)
                for h, half in enumerate(HALVES):
                    for k in range(KT - 1):
                        pool.wait_ge(sq_ready, sq_base(n) + KT * h + k + 1)
                        pool.wait_ge(acc_done, acc_base(n) + (KT - 1) * h + k + 1)
                        pool.tensor_tensor(acc[:, half], acc[:, half], sq[:, k % 2, half], ALU.add).then_inc(acc_done, 1)

            for q in range(min(n_sub, CONV_SUB + 1)):
                pre_norm_sums(q)
                if SUBLAYERS[q][0] == "sgu":
                    pool.wait_ge(spatial_loaded, 16)
                    pool.affine_select(out=ws_raw[:], in_=ws_raw[:], compare_op=ALU.is_ge, fill=0.0, base=0,
                                       pattern=[[0, GROUPS], [1, CHUNK]], channel_multiplier=-1).then_inc(spatial_masked, 1)
                    pool.wait_ge(v_ln, 4)
                    for g in range(GROUPS):
                        for c in range(NC):
                            pool.tensor_scalar(v_tok[:, g, c, :], v_tok[:, g, c, :], v_inv[:, c, :], v_off[:, c, :],
                                               ALU.mult, ALU.add).then_inc(v_normed, 1)
            if n_sub > CONV_SUB:
                adds = len(POOL_TAPS) - 1

                def statistics(t):
                    pool.wait_ge(conv_sq, t + 1)
                    if t == 1:
                        pool.tensor_tensor(acc[:], conv_y[:, 0, :], conv_y[:, 1, :], ALU.add).then_inc(conv_sq_free, 1)
                        pool.tensor_tensor(sq_sum[:], sq[:, 0, :], sq[:, 1, :], ALU.add).then_inc(conv_sq_free, 1)
                    elif t > 1:
                        pool.wait_ge(conv_sq_free, 2 * t + 2)
                        pool.tensor_tensor(acc[:], acc[:], conv_y[:, t, :], ALU.add).then_inc(conv_sq_free, 1)
                        pool.tensor_tensor(sq_sum[:], sq_sum[:], sq[:, t % 2, :], ALU.add).then_inc(conv_sq_free, 1)
                pool.wait_ge(product_ready, 1)
                pool.memset(sq_sum[:], 0.0).then_inc(conv_sq_free, 4)
                for t in range(KT):
                    if t in (2, 3):
                        pool.wait_ge(neg_c_ready, 1)
                        pool.wait_ge(conv_part, 3 * (t - 1))
                        pool.tensor_tensor(conv_y[:, t - 2, :], conv_y[:, t - 2, :], neg_c[:], ALU.add).then_inc(shifted, 1)
                    if t >= 3:
                        statistics(t - 2)
                    for n in range(adds):
                        pool.wait_ge(product_ready, t * (adds + 1) + n + 2)
                        if t or n:
                            pool.wait_ge(pool_sum, t * adds + n)
                        pool.tensor_tensor(pool_acc[:, t % 2, :], pool_acc[:, t % 2, :],
                                           tap_product[:, (t * adds + n) % PRODUCTS, :], ALU.add).then_inc(pool_sum, 1)
                for q in range(CONV_SUB + 1, n_sub):
                    pre_norm_sums(q)

            for h, half in enumerate(HALVES):
                for k in range(1, KT, 2):
                    pool.wait_ge(y_scaled, 2 * KT * (n_sub - 1) + KT * h + k + 1)
                    pool.tensor_tensor(x_fm[:, k, half], x_fm[:, k, half], y_out[:, k, half],
                                       ALU.add).then_inc(odd_x_ready, 1)

        @block.scalar
        def _(act):
            act.dma_start(par[:], params).then_inc(param_loaded, 16)
            act.preload_act_table(ACT.Sqrt)

            def settle():
                act.wait_ge(param_loaded, 16)

            def split_hi(s_static, i, stride, p, cols):
                if not cols:
                    return
                act.wait_ge(raw_loaded[p], 16 * (s_static // 2 + 1) + 16 * (stride // 2) * i)
                if s_static >= 2 or not isinstance(i, int):
                    act.wait_ge(step_used, s_static - 1 + stride * i)
                act.activation(w_hi[:, p, 0:cols], w_raw[:, p, 0:cols], ACT.Copy).then_inc(hi_done, 1)

            def hi_of_first_piece(j):
                if j < PIECES - 1:
                    act.wait_ge(piece_loaded[0][j], 16)
                else:
                    act.wait_ge(raw_loaded[0], 16)
                at = slice(j * PIECE, (j + 1) * PIECE)
                act.activation(w_hi[:, 0, at], w_raw[:, 0, at],
                               ACT.Copy).then_inc(first_hi if j < PIECES - 1 else hi_done, 1)

            def hi_of_piece(s, j):
                at = slice(j * PIECE, (j + 1) * PIECE)
                act.activation(w_hi[:, s % 2, at], w_raw[:, s % 2, at],
                               ACT.Copy).then_inc(hi_piece if j < PIECES - 1 else hi_done, 1)

            def root_of(n, h=0, columns=slice(0, NC)):
                act.wait_ge(ms_ready, trip(n, h) + 1)
                act.activation(root[:, columns], stat[:, columns], ACT.Sqrt).then_inc(root_ready, 1)

            def last_half_squares(q, h, s_end):
                n, half = post_norm(q), HALVES[h]
                if h:
                    act.wait_ge(step_used, s_end)
                else:
                    act.wait_ge(last_half, q + 1)
                    act.wait_ge(acc_done, acc_base(n) + KT - 1)
                act.activation(sq[:, 1, half], bank[LAST_BANKS[h]][:, half], ACT.Square).then_inc(sq_ready, 1)

            def last_half_copy(h):
                half = HALVES[h]
                ins = act.activation(y_out[:, KT - 1, half], bank[LAST_BANKS[h]][:, half], ACT.Copy)
                if h:
                    ins.then_inc(out_bank_free, 1)

            def second_root(q):
                root_of(post_norm(q), 1, slice(NC // 2, NC))

            def diagonal(i, p, n, part):
                dst, w, j = (tap_hi, tap_lo)[part], (dwh, dwl)[part], PE_TAPS[n]
                act.activation(dst[:, p, n, :], ident[:], ACT.Identity,
                               scale=w[:, i, p, j:j + 1]).then_inc(diag_built, 1)

            def prepare_x(q, s0):
                n, row = pre_norm(q), SUBLAYERS[q][1]
                if q:
                    last_half_squares(q - 1, 1, s0)
                for h, half in enumerate(HALVES):
                    for k in range(KT):
                        if q == 0:
                            if h == 0 and k % 2 == 0:
                                hi_of_first_piece(k // 2)
                            if h == 0 and k == 0:
                                act.wait_ge(param_loaded, 16)
                            if k % X_TILES == 0:
                                act.wait_ge(x_loaded[h][k // X_TILES], 16)
                        else:
                            if h == 0 and k == 2:
                                second_root(q - 1)
                            act.wait_ge(x_ready, 2 * KT * (q - 1) + KT * h + k + 1)
                        act.activation(xn_hi[:, k, half], x_fm[:, k, half], ACT.Identity,
                                       scale=gain[:, row, k:k + 1]).then_inc(xhi_ready, 1)
                        if h == 0 and k % 2 == 0:
                            if q == 0 and k // 2 < PIECES - 1:
                                act.wait_ge(piece_loaded[1][k // 2], 16)
                            elif q == 0 or k == 0:
                                act.wait_ge(raw_loaded[1], 16 * (s0 // 2 + 1))
                            hi_of_piece(s0 + 1, k // 2)
                        if q and h == 0 and k == 0:
                            last_half_copy(1)
                        if k >= 2:
                            act.wait_ge(acc_done, acc_base(n) + (KT - 1) * h + k)
                        act.activation(sq[:, k % 2, half], x_fm[:, k, half], ACT.Square).then_inc(sq_ready, 1)
                        if q == CONV_SUB and h:
                            for part in range(2):
                                diagonal(0, 0, k, part)
                    if q == CONV_SUB and h == 0:
                        act.activation(dw_hi[:], dw_all, ACT.Copy).then_inc(dw_hi_ready, 1)
                        act.wait_ge(dw_ready, 1)
                for j in range(PIECES - 1):
                    for m in (2, 3):
                        if j == 0:
                            act.wait_ge(raw_loaded[m % 2], 16 * (s0 // 2 + 2))
                        act.wait_ge(cols_used, (PIECES - 1) * q + j + 1)
                        hi_of_piece(s0 + m, j)
                root_of(n)
                act.preload_act_table(IN_FUNCTION[SUBLAYERS[q][0]])
                act.wait_ge(step_used, s0 + 2)
                for m in (2, 3):
                    hi_of_piece(s0 + m, PIECES - 1)
                act.wait_ge(cast_ready, trip(n) + 1)
                act.activation(rms_inv[:], bank[CAST][:], ACT.Copy).then_inc(rms_ready, 1)

            def evacuate(d_sq, e_static, e_dyn, n, dst, src):
                act.wait_ge(acc_done, acc_base(n) + e_static + e_dyn)
                act.activation(sq[:, d_sq, :], src, ACT.Square).then_inc(sq_ready, 1)
                act.activation(dst, src, ACT.Copy).then_inc(out_bank_free, 1)

            h_hi_p = h_hi[:].rearrange("p (i t) n -> p i t n", t=2)
            y_p = y_out[:].rearrange("p (i t) n -> p i t n", t=2)
            act.wait_ge(const_ready, 2)
            act.activation(root[:, 0, :], eps[:], ACT.Copy).then_inc(out_bank_free, 2)
            for ph in phases:
                s0, n_pairs, kind, q = ph.s0, ph.steps // 2, ph.kind, ph.sub
                if kind in ("ffn_in", "v", "conv_in"):
                    prepare_x(q, s0)
                elif kind != "u":
                    act.preload_act_table(ACT.Sqrt)

                if kind == "ffn_in":
                    def body(i, cols):
                        for p in range(2):
                            act.wait_ge(scaled, 2 * ph.in0 + 2 * p + 1 + 4 * i)
                            act.activation(first[:, p, :], first[:, p, :], ACT.Silu).then_inc(act_done, 1)
                            if not isinstance(i, int) or i:
                                split_hi(s0 + 2 + p, i, 2, p, cols)
                            act.wait_ge(prod_ready, ph.prod0 + p + 1 + 2 * i)
                            settle()
                            act.activation(h_hi_p[:, i, p, :], second[:, p, :], ACT.Copy).then_inc(prod_hi, 1)
                    body(0, 0)
                    with pairs(act, 1, n_pairs - 1) as i:
                        body(i, ph.cols)
                    body(n_pairs - 1, ph.next_cols)

                elif kind == "ffn_out":
                    n = post_norm(q)

                    def body(i, cols):
                        for d in range(2):
                            last = cols != ph.cols and d == 1
                            c = cols if last else ph.cols
                            split_hi(s0 + 2 * d + 2, i, 4, 0, c)
                            if not last:
                                act.wait_ge(step_used, s0 + 2 * d + 2 + 4 * i)
                                evacuate(d, d, 2 * i, n, y_p[:, i, d, :], bank[OUT_BANKS[d]][:])
                                split_hi(s0 + 2 * d + 3, i, 4, 1, c)
                    with pairs(act, 0, n_pairs // 2 - 1) as i:
                        body(i, ph.cols)
                    body(n_pairs // 2 - 1, ph.next_cols)

                elif kind == "v":
                    vt = v_tok[:].rearrange("p (i t) c d -> p i t c d", t=2)
                    act.wait_ge(spatial_masked, 1)
                    act.activation(ws_hi[:], ws_raw[:], ACT.Copy).then_inc(ws_hi_ready, 1)

                    def copies(dst, t_static, i):
                        for j in range(2):
                            act.wait_ge(v_turned, t_static * 2 + j + 1 + 4 * i)
                            settle()
                            act.activation(dst[:, :, j * P:(j + 1) * P],
                                           bank[MIX_BANKS[j]][:].rearrange("p (c d) -> p c d", d=P),
                                           ACT.Copy).then_inc(v_copied, 1)

                    def body(i, peeled):
                        for p in range(2):
                            for j, buf in enumerate((first, second)):
                                act.wait_ge(scaled, 2 * ph.in0 + 2 * p + j + 1 + 4 * i)
                                act.activation(buf[:, p, :], buf[:, p, :], ACT.Gelu_apprx_tanh).then_inc(act_done, 1)
                            if not peeled:
                                split_hi(s0 + 2 + p, i, 2, p, ph.cols)
                            if p:
                                copies(vt[:, i, 0], 0, i)
                            elif not peeled:
                                copies(vt[:, i - 1, 1], -1, i)
                    body(0, True)
                    with pairs(act, 1, n_pairs) as i:
                        body(i, False)
                    act.wait_ge(rowsum_mm, 1)
                    for j in range(2):
                        act.activation(ws_rowsum[:, 4 * j:4 * j + 4, :],
                                       bank[OUT_BANKS[j]][:].rearrange("p (g t) -> p g t", t=CHUNK),
                                       ACT.Copy).then_inc(rowsum_ready, 1)
                    copies(vt[:, n_pairs - 1, 1], 2 * n_pairs - 1, 0)
                    act.wait_ge(v_ln, 2)
                    act.activation(v_root[:], v_var[:], ACT.Sqrt).then_inc(v_rooted, 1)

                elif kind == "u":
                    vt = v_tok[:].rearrange("p (i t) c d -> p i t c d", t=2)
                    gt = gated[:].rearrange("p (i g) h t n -> p i g h t n", g=2)

                    def body(i):
                        for p in range(2):
                            if p or not isinstance(i, int):
                                act.wait_ge(mix_ready, p + 2 * i)
                            act.wait_ge(v_normed, NC * (p + 1) + 2 * NC * i)
                            settle()
                            act.activation(vs_hi[:], vt[:, i, p], ACT.Copy).then_inc(vs_hi_ready, 1)
                            for j, buf in enumerate((first, second)):
                                act.wait_ge(scaled, 2 * ph.in0 + 2 * p + j + 1 + 4 * i)
                                act.activation(buf[:, p, :], buf[:, p, :], ACT.Gelu_apprx_tanh).then_inc(act_done, 1)
                            split_hi(s0 + 2 + p, i, 2, p, ph.cols)
                            for j, buf in enumerate((first, second)):
                                act.wait_ge(prod_ready, ph.prod0 + 2 * p + j + 1 + 4 * i)
                                settle()
                                act.activation(gt[:, i, p, 0, j, :], buf[:, p, :], ACT.Copy).then_inc(prod_hi, 1)
                    body(0)
                    with pairs(act, 1, n_pairs) as i:
                        body(i)

                elif kind == "sgu_out":
                    n = post_norm(q)

                    def body(i, last):
                        for d in range(1 if last else 2):
                            act.wait_ge(step_used, s0 + d + 1 + 2 * i)
                            evacuate(d, d, 2 * i, n, y_p[:, i, d, :], bank[OUT_BANKS[d]][:])
                            split_hi(s0 + 2 + d, i, 2, d, ph.next_cols if last else ph.cols)
                    with pairs(act, 0, n_pairs - 1) as i:
                        body(i, False)
                    body(n_pairs - 1, True)

                elif kind == "conv_in":
                    adds = len(POOL_TAPS) - 1
                    assert 2 * adds % PRODUCTS == 0

                    def products(i, p, ns, last=False):
                        later = not isinstance(i, int) or i > 0
                        for n in ns:
                            if 0 < n <= len(PE_TAPS) and not last:
                                for part in range(2):
                                    diagonal(i + p, 1 - p, n - 1, part)
                            j = POOL_TAPS[n]
                            if n == 0:
                                if later:
                                    act.wait_ge(conv_part, 3 * (p - 1) + 6 * i)
                                    settle()
                                act.activation(pool_acc[:, p, :], conv_pad[:, p, j:j + T], ACT.Identity,
                                               scale=dw[:, i, p, j:j + 1],
                                               bias=dw_b[:, i, p:p + 1]).then_inc(product_ready, 1)
                                continue
                            m = p * adds + n - 1
                            if later or m >= PRODUCTS:
                                act.wait_ge(pool_sum, m - PRODUCTS + 1 + 2 * adds * i)
                                settle()
                            act.activation(tap_product[:, m % PRODUCTS, :], conv_pad[:, p, j:j + T],
                                           ACT.Identity, scale=dw[:, i, p, j:j + 1]).then_inc(product_ready, 1)

                    def tile_squares(k):
                        act.wait_ge(conv_part, 3 * (k + 1))
                        act.wait_ge(conv_sq_free, 2 * KT - 2)
                        act.activation(sq[:, k % 2, :], conv_y[:, k, :], ACT.Square).then_inc(conv_sq, 1)

                    def body(i, last=False):
                        later = not isinstance(i, int) or last
                        for p in range(2):
                            act.wait_ge(scaled, 2 * ph.in0 + 2 * p + 1 + 4 * i)
                            act.activation(first[:, p, :], first[:, p, :], ACT.Sigmoid).then_inc(act_done, 1)
                            if later:
                                act.wait_ge(shifted, p + 1)
                                act.wait_ge(conv_part, 3 * (p - 1) + 6 * i)
                                act.wait_ge(conv_sq_free, 4 * i + 2 * p - 2)
                                settle()
                                act.activation(sq[:, p, :], cy[:, i - 1, p, :], ACT.Square).then_inc(conv_sq, 1)
                            act.wait_ge(conv_in_ready, p + 1 + 2 * i)
                            if later or p:
                                act.wait_ge(pe_taps, p + 2 * i)
                                settle()
                            act.activation(pad_hi[:, p, :], conv_pad[:, p, :], ACT.Copy).then_inc(pad_hi_ready, 1)
                            products(i, p, range(SPLIT_AFTER), last and p)
                            if later:
                                split_hi(s0 + 2 + p, i, 2, p, ph.cols)
                            products(i, p, range(SPLIT_AFTER, len(PE_TAPS)), last and p)
                            if last and p:
                                tile_squares(KT - 2)
                            products(i, p, range(len(PE_TAPS), len(POOL_TAPS)), last and p)
                    cy = conv_y[:].rearrange("p (i t) n -> p i t n", t=2)
                    body(0)
                    act.wait_ge(c_ready, 1)
                    act.activation(neg_c[:], bank[TAP_BANKS[0]][:], ACT.Copy, scale=-1.0 / P).then_inc(neg_c_ready, 1)
                    with pairs(act, 1, n_pairs - 1) as i:
                        body(i)
                    body(n_pairs - 1, True)
                    tile_squares(KT - 1)
                    act.preload_act_table(ACT.Sqrt)
                    act.wait_ge(ln_step, 3)
                    act.activation(root[:], stat[:, 0:NC], ACT.Sqrt, scale=1.0 / D_MODEL, bias=eps[:, 0:1]).then_inc(ln_root, 1)
                    act.preload_act_table(ACT.Silu)
                    for k in range(KT):
                        act.wait_ge(conv_scaled, k + 1)
                        act.activation(conv_y[:, k, :], conv_y[:, k, :], ACT.Silu, scale=cln_g[:, k:k + 1],
                                       bias=cln_b[:, k:k + 1]).then_inc(prod_ready, 1)
                        act.wait_ge(prod_ready, ph.prod0 + k + 1)
                        act.activation(conv_hi[:, k, :], conv_y[:, k, :], ACT.Copy).then_inc(prod_hi, 1)

                elif kind == "conv_out":
                    n = post_norm(q)

                    def body(i, cols):
                        for p in range(2):
                            for d in range(2):
                                if i and p and d:
                                    continue
                                if d == 0:
                                    act.wait_ge(half_step, p + 1 + 2 * i)
                                else:
                                    act.wait_ge(step_used, s0 + p + 1 + 2 * i)
                                evacuate(d, 2 * p + d, 4 * i, n,
                                         y_out[:].rearrange("p (i t) n -> p i t n", t=4)[:, i, 2 * p + d, :],
                                         bank[CONV_OUT_BANKS[4 * i + 2 * p + d]][:])
                            if not (i and p):
                                split_hi(s0 + 2 + p, i, 2, p, cols)
                    body(0, ph.cols)
                    body(1, ph.next_cols)

                if kind in ("ffn_out", "sgu_out", "conv_out"):
                    last_half_squares(q, 0, s0 + ph.steps)
                    last_half_copy(0)
                    root_of(post_norm(q), 0, slice(0, NC // 2))
                    if q + 1 == n_sub:
                        last_half_squares(q, 1, s0 + ph.steps)
                        last_half_copy(1)
                        second_root(q)

        @block.vector
        def _(dve):
            def split_lo(s_static, i, stride, p, cols):
                if not cols:
                    return
                dve.wait_ge(hi_done, s_static + 1 + stride * i)
                dve.tensor_tensor(w_lo[:, p, 0:cols], w_raw[:, p, 0:cols], w_hi[:, p, 0:cols].bitcast(F32),
                                  ALU.subtract).then_inc(split_done, 1)

            def lo_of_first_piece(j):
                if j < PIECES - 1:
                    dve.wait_ge(first_hi, j + 1)
                else:
                    dve.wait_ge(hi_done, 1)
                at = slice(j * PIECE, (j + 1) * PIECE)
                dve.tensor_tensor(w_lo[:, 0, at], w_raw[:, 0, at], w_hi[:, 0, at].bitcast(F32),
                                  ALU.subtract).then_inc(first_lo if j < PIECES - 1 else split_done, 1)

            def lo_of_piece(q, s0, m, j):
                if j == PIECES - 1:
                    dve.wait_ge(hi_done, s0 + m + 1)
                else:
                    count = j + 1 if m == 1 else PIECES - 1 + 2 * j + m - 1
                    dve.wait_ge(hi_piece, 3 * (PIECES - 1) * q + count)
                at, slot = slice(j * PIECE, (j + 1) * PIECE), m % 2
                dve.tensor_tensor(w_lo[:, slot, at], w_raw[:, slot, at], w_hi[:, slot, at].bitcast(F32),
                                  ALU.subtract).then_inc(lo_piece if j < PIECES - 1 else split_done, 1)

            def clear_acc(n):
                dve.memset(acc[:], 0.0).then_inc(acc_done, 1)

            def add_sq(n, e_static, e_dyn, slot):
                dve.wait_ge(sq_ready, sq_base(n) + e_static + 1 + e_dyn)
                dve.wait_ge(acc_done, acc_base(n) + e_static + 1 + e_dyn)
                dve.tensor_tensor(acc[:], acc[:], sq[:, slot, :], ALU.add).then_inc(acc_done, 1)

            def columns(b, lo, hi):
                return bank[b][:, lo:hi].rearrange("p (c o) -> p c o", o=1)

            def mean_square(n, h=0, cs=slice(0, NC)):
                if h == 0:
                    dve.wait_ge(stat_part_ready, n + 1)
                    dve.tensor_scalar(stat_part[:, 0:NC], columns(CAST, 0, NC), 1.0 / D_MODEL, EPS,
                                      ALU.mult, ALU.add).then_inc(part_ready, 1)
                    dve.wait_ge(part_ready, n + 1)
                dve.wait_ge(stat_ready, trip(n, h) + 1)
                dve.scalar_tensor_tensor(out=stat[:, cs], in0=columns(STAT, cs.start, cs.stop), scalar=1.0 / D_MODEL,
                                         in1=stat_part[:, cs], op0=ALU.mult, op1=ALU.add).then_inc(ms_ready, 1)

            def inverse(n, h=0, cs=slice(0, NC)):
                dve.wait_ge(root_ready, trip(n, h) + 1)
                dve.reciprocal(inv[:, cs], root[:, cs]).then_inc(inv_ready, 1)
                dve.wait_ge(inv_ready, trip(n, h) + 1)
                diagonal(diag_ready, cs)

            def diagonal(signal, cs=slice(0, NC)):
                shape = [P, cs.stop - cs.start, P]
                dve.tensor_tensor(diag[:, cs], ident[:].rearrange("p (o n) -> p o n", o=1).broadcast_to(shape),
                                  inv[:, cs].broadcast_to(shape), ALU.mult).then_inc(signal, 1)

            def residual_and_prepare(q_done, q_next, s0):
                row_y = SUBLAYERS[q_done][2] if q_done is not None else None
                row_x, n = SUBLAYERS[q_next][1], pre_norm(q_next)
                if q_done is not None:
                    g_y = half_g if SUBLAYERS[q_done][0] == "ffn" else gain
                later_tokens = slice(NC // 2, NC)

                def normed(h, k):
                    dve.tensor_tensor(y_out[:, k, HALVES[h]], y_out[:, k, HALVES[h]], bank[CAST_HALVES[h]][:, HALVES[h]],
                                      ALU.mult).then_inc(y_scaled, 1)

                for h, half in enumerate(HALVES):
                    if q_done is not None:
                        dve.wait_ge(cast_ready, trip(post_norm(q_done), h) + 1)
                    for k in range(KT + 1):
                        if q_done is None and h == 0 and k < KT and k % 2 == 0:
                            lo_of_first_piece(k // 2)
                        if q_done is not None and k < KT:
                            if k == 0:
                                normed(h, 0)
                            if h == 0 and k == 2:
                                mean_square(post_norm(q_done), 1, later_tokens)
                            dve.wait_ge(y_scaled, 2 * KT * q_done + KT * h + k + 1)
                            dve.scalar_tensor_tensor(out=x_fm[:, k, half], in0=y_out[:, k, half],
                                                     scalar=g_y[:, row_y, k:k + 1], in1=x_fm[:, k, half],
                                                     op0=ALU.mult, op1=ALU.add).then_inc(x_ready, 1)
                            if h == 0 and k == 2:
                                inverse(post_norm(q_done), 1, later_tokens)
                            if k + 1 < KT:
                                normed(h, k + 1)
                        if k >= 1:
                            j = k - 1
                            dve.wait_ge(xhi_ready, 2 * KT * q_next + KT * h + j + 1)
                            dve.scalar_tensor_tensor(out=xn_lo[:, j, half], in0=x_fm[:, j, half],
                                                     scalar=gain[:, row_x, j:j + 1], in1=xn_hi[:, j, half].bitcast(F32),
                                                     op0=ALU.mult, op1=ALU.subtract).then_inc(xlo_ready, 1)
                        if h == 0 and k < KT and k % 2 == 0:
                            lo_of_piece(q_next, s0, 1, k // 2)
                    if q_next == CONV_SUB and h == 0:
                        dve.wait_ge(dw_hi_ready, 1)
                        dve.tensor_tensor(dw_lo[:], dw_all, dw_hi[:].bitcast(F32), ALU.subtract).then_inc(dw_ready, 1)
                for j in range(PIECES - 1):
                    for m in (2, 3):
                        lo_of_piece(q_next, s0, m, j)
                mean_square(n)
                inverse(n)
                for m in (2, 3):
                    lo_of_piece(q_next, s0, m, PIECES - 1)

            def last_residual(q):
                n = post_norm(q)
                g_y, row_y = half_g if SUBLAYERS[q][0] == "ffn" else gain, SUBLAYERS[q][2]
                for h, half in enumerate(HALVES):
                    dve.wait_ge(cast_ready, trip(n, h) + 1)
                    for k in range(KT):
                        if h == 0 and k == 2:
                            mean_square(n, 1, slice(NC // 2, NC))
                        if h == 0 and k == 3:
                            inverse(n, 1, slice(NC // 2, NC))
                        dve.scalar_tensor_tensor(out=y_out[:, k, half], in0=y_out[:, k, half], scalar=g_y[:, row_y, k:k + 1],
                                                 in1=bank[CAST_HALVES[h]][:, half], op0=ALU.mult,
                                                 op1=ALU.mult).then_inc(y_scaled, 1)
                        if k % 2:
                            dve.wait_ge(y_scaled, 2 * KT * q + KT * h + k)
                            dve.tensor_tensor(x_fm[:, k - 1, half], x_fm[:, k - 1, half], y_out[:, k - 1, half],
                                              ALU.add).then_inc(x_ready, 1)

            def scale_banks(ph, i, p, banks, j):
                if j == 0:
                    dve.wait_ge(proj_ready, ph.in0 + p + 1 + 2 * i)
                else:
                    dve.wait_ge(step_used, ph.s0 + p + 1 + 2 * i)
                dve.tensor_tensor((first, second)[j][:, p, :], bank[banks[p][j]][:], rms_inv[:],
                                  ALU.mult).then_inc(scaled, 1)

            h_hi_p = h_hi[:].rearrange("p (i t) n -> p i t n", t=2)
            h_lo_p = h_lo[:].rearrange("p (i t) n -> p i t n", t=2)
            dve.wait_ge(param_loaded, 16)
            dve.tensor_scalar(half_g[:], gain, 0.5, None, ALU.mult).then_inc(half_ready, 1)
            dve.wait_ge(half_ready, 1)
            dve.wait_ge(const_ready, 4)
            residual_and_prepare(None, 0, 0)
            for ph in phases:
                s0, n_pairs, kind, q = ph.s0, ph.steps // 2, ph.kind, ph.sub
                if kind in ("ffn_in", "v", "conv_in"):
                    dve.wait_ge(rms_ready, q + 1)

                if kind == "ffn_in":
                    def body(i, banks, cols):
                        for p in range(2):
                            scale_banks(ph, i, p, banks, 0)
                            scale_banks(ph, i, p, banks, 1)
                            dve.wait_ge(act_done, ph.act0 + p + 1 + 2 * i)
                            dve.wait_ge(scaled, 2 * ph.in0 + 2 * p + 2 + 4 * i)
                            dve.tensor_tensor(second[:, p, :], second[:, p, :], first[:, p, :],
                                              ALU.mult).then_inc(prod_ready, 1)
                            if not isinstance(i, int) or i:
                                split_lo(s0 + 2 + p, i, 2, p, cols)
                            dve.wait_ge(prod_hi, ph.prod0 + p + 1 + 2 * i)
                            dve.tensor_tensor(h_lo_p[:, i, p, :], second[:, p, :], h_hi_p[:, i, p, :].bitcast(F32),
                                              ALU.subtract).then_inc(prod_lo, 1)
                    body(0, FIRST_BANKS, ph.cols)
                    with pairs(dve, 1, n_pairs - 1) as i:
                        body(i, IN_BANKS, ph.cols)
                    body(n_pairs - 1, IN_BANKS, ph.next_cols)

                elif kind == "ffn_out":
                    n = post_norm(q)
                    clear_acc(n)

                    def body(i, cols):
                        for d in range(2):
                            last = cols != ph.cols
                            c = cols if last and d == 1 else ph.cols
                            split_lo(s0 + 2 * d + 2, i, 4, 0, c)
                            if not (last and d == 1):
                                add_sq(n, d, 2 * i, d)
                            if not (last and d == 1):
                                split_lo(s0 + 2 * d + 3, i, 4, 1, c)
                    with pairs(dve, 0, n_pairs // 2 - 1) as i:
                        body(i, ph.cols)
                    body(n_pairs // 2 - 1, ph.next_cols)

                elif kind == "v":
                    vt = v_tok[:].rearrange("p (i t) c d -> p i t c d", t=2)
                    vst = v_stats[:].rearrange("p c (i t) s -> p i t c s", t=2)
                    dve.wait_ge(ws_hi_ready, 1)
                    dve.tensor_tensor(ws_lo[:], ws_raw[:], ws_hi[:].bitcast(F32), ALU.subtract).then_inc(ws_ready, 1)

                    def stats(src, dst, t_static, i):
                        dve.wait_ge(v_copied, 2 * t_static + 2 + 4 * i)
                        for c in range(NC):
                            ins = dve.bn_stats(out=dst[:, c, :], in_=src[:, c, :])
                        ins.then_inc(v_stats_done, 1)

                    def body(i, banks, peeled):
                        for p in range(2):
                            if not peeled:
                                dve.wait_ge(v_turned, 2 * p - 2 + 4 * i)
                            scale_banks(ph, i, p, banks, 0)
                            scale_banks(ph, i, p, banks, 1)
                            if not peeled:
                                split_lo(s0 + 2 + p, i, 2, p, ph.cols)
                            if p:
                                stats(vt[:, i, 0], vst[:, i, 0], 0, i)
                            elif not peeled:
                                stats(vt[:, i - 1, 1], vst[:, i - 1, 1], -1, i)
                    body(0, FIRST_BANKS, True)
                    with pairs(dve, 1, n_pairs) as i:
                        body(i, IN_BANKS, False)
                    stats(vt[:, n_pairs - 1, 1], vst[:, n_pairs - 1, 1], 2 * n_pairs - 1, 0)
                    dve.wait_ge(v_stats_done, GROUPS)
                    for c in range(NC):
                        ins = dve.bn_aggr(out=v_mv[:, c, :], in_=v_stats[:, c, :, :].rearrange("p g s -> p (g s)"))
                    ins.then_inc(v_ln, 1)
                    dve.wait_ge(v_ln, 1)
                    dve.tensor_scalar(v_var[:], v_mv[:, :, 1:2], EPS, None, ALU.add).then_inc(v_ln, 1)
                    dve.wait_ge(v_rooted, 1)
                    dve.reciprocal(v_inv[:], v_root[:]).then_inc(v_ln, 1)
                    dve.wait_ge(v_ln, 3)
                    dve.scalar_tensor_tensor(out=v_off[:], in0=v_mv[:, :, 0:1], scalar=-1.0, in1=v_inv[:],
                                             op0=ALU.mult, op1=ALU.mult).then_inc(v_ln, 1)

                elif kind == "u":
                    vt = v_tok[:].rearrange("p (i t) c d -> p i t c d", t=2)
                    gt = gated[:].rearrange("p (i g) h t n -> p i g h t n", g=2)
                    rs = ws_rowsum[:].rearrange("p (i g) t -> p i g t", g=2)
                    bs = ws_bias[:].rearrange("p (i g) t -> p i g t", g=2)
                    dve.wait_ge(rowsum_ready, 2)
                    dve.wait_ge(bias_loaded, 16)

                    def body(i):
                        for p in range(2):
                            dve.wait_ge(vs_hi_ready, p + 1 + 2 * i)
                            dve.tensor_tensor(vs_lo[:], vt[:, i, p], vs_hi[:].bitcast(F32),
                                              ALU.subtract).then_inc(vs_ready, 1)
                            for j in range(GT):
                                dve.scalar_tensor_tensor(out=shift[:, j, :], in0=rs[:, i, p, :],
                                                         scalar=sgu_b[:, i, p, j:j + 1], in1=bs[:, i, p, :],
                                                         op0=ALU.mult, op1=ALU.add).then_inc(shift_ready, 1)
                            scale_banks(ph, i, p, IN_BANKS, 0)
                            scale_banks(ph, i, p, IN_BANKS, 1)
                            split_lo(s0 + 2 + p, i, 2, p, ph.cols)
                            dve.wait_ge(mix_ready, p + 1 + 2 * i)
                            dve.wait_ge(shift_ready, 2 * p + 2 + 4 * i)
                            for j in range(GT):
                                dve.scalar_tensor_tensor(
                                    out=mixed[:, j, :].rearrange("p (c t) -> p c t", t=CHUNK),
                                    in0=bank[MIX_BANKS[j]][:].rearrange("p (c t) -> p c t", t=CHUNK),
                                    scalar=sgu_g[:, i, p, j:j + 1],
                                    in1=shift[:, j:j + 1, :].broadcast_to([P, NC, CHUNK]),
                                    op0=ALU.mult, op1=ALU.add).then_inc(mixed_ready, 1)
                            for j, buf in enumerate((first, second)):
                                dve.wait_ge(act_done, ph.act0 + 2 * p + j + 1 + 4 * i)
                                dve.wait_ge(mixed_ready, 2 * p + j + 1 + 4 * i)
                                dve.tensor_tensor(buf[:, p, :], buf[:, p, :], mixed[:, j, :],
                                                  ALU.mult).then_inc(prod_ready, 1)
                            for j, buf in enumerate((first, second)):
                                dve.wait_ge(prod_hi, ph.prod0 + 2 * p + j + 1 + 4 * i)
                                dve.tensor_tensor(gt[:, i, p, 1, j, :], buf[:, p, :], gt[:, i, p, 0, j, :].bitcast(F32),
                                                  ALU.subtract).then_inc(prod_lo, 1)
                    with pairs(dve, 0, n_pairs) as i:
                        body(i)

                elif kind == "sgu_out":
                    n = post_norm(q)
                    clear_acc(n)

                    def body(i, last):
                        for d in range(2):
                            if not (last and d == 1):
                                add_sq(n, d, 2 * i, d)
                            if not (last and d == 1):
                                split_lo(s0 + 2 + d, i, 2, d, ph.next_cols if last else ph.cols)
                    with pairs(dve, 0, n_pairs - 1) as i:
                        body(i, False)
                    body(n_pairs - 1, True)

                elif kind == "conv_in":
                    cy = conv_y[:].rearrange("p (i t) n -> p i t n", t=2)
                    dve.memset(conv_pad[:, :, 0:PAD], 0.0).then_inc(pad_zeroed, 1)
                    dve.wait_ge(pad_zeroed, 1)
                    n_dve, n_products = len(DVE_TAPS), len(POOL_TAPS)

                    def put_together(y, p, t, i):
                        dve.wait_ge(tap_done, n_dve * (t + 1) + 2 * n_dve * i)
                        dve.tensor_tensor(y, bank[ODD][:], even_sum[:], ALU.add).then_inc(conv_part, 1)
                        dve.wait_ge(conv_part, 3 * t + 1 + 6 * i)
                        dve.wait_ge(pe_taps, t + 1 + 2 * i)
                        dve.tensor_tensor(y, bank[TAP_BANKS[p]][:], y, ALU.add).then_inc(conv_part, 1)

                    def add_pool_sum(y, p, t, i):
                        dve.wait_ge(pool_sum, (n_products - 1) * (t + 1) + 2 * (n_products - 1) * i)
                        dve.wait_ge(conv_part, 3 * t + 2 + 6 * i)
                        dve.tensor_tensor(y, y, pool_acc[:, p, :], ALU.add).then_inc(conv_part, 1)

                    def body(i, banks):
                        later = not isinstance(i, int)
                        for p in range(2):
                            scale_banks(ph, i, p, banks, 0)
                            scale_banks(ph, i, p, banks, 1)
                            dve.wait_ge(act_done, ph.act0 + p + 1 + 2 * i)
                            dve.wait_ge(scaled, 2 * ph.in0 + 2 * p + 2 + 4 * i)
                            if later:
                                dve.wait_ge(pe_taps, p - 1 + 2 * i)
                                dve.wait_ge(product_ready, n_products * (p - 1) + 2 * n_products * i)
                            dve.tensor_tensor(conv_pad[:, p, PAD:], first[:, p, :], second[:, p, :],
                                              ALU.mult).then_inc(conv_in_ready, 1)
                            if p:
                                put_together(cy[:, i, 0, :], 0, 0, i)
                            elif later:
                                put_together(cy[:, i - 1, 1, :], 1, -1, i)
                            dve.wait_ge(conv_in_ready, p + 1 + 2 * i)
                            for n, j in enumerate(DVE_TAPS):
                                if n == PAD_SPLIT_AFTER:
                                    dve.wait_ge(pad_hi_ready, p + 1 + 2 * i)
                                    dve.tensor_tensor(pad_lo[:, p, :], conv_pad[:, p, :], pad_hi[:, p, :].bitcast(F32),
                                                      ALU.subtract).then_inc(pad_ready, 1)
                                if n == POOL_SUM_AFTER and p:
                                    add_pool_sum(cy[:, i, 0, :], 0, 0, i)
                                elif n == POOL_SUM_AFTER and later:
                                    add_pool_sum(cy[:, i - 1, 1, :], 1, -1, i)
                                if later and n == SPLIT_AFTER:
                                    split_lo(s0 + 2 + p, i, 2, p, ph.cols)
                                dst, src, w = bank[ODD][:] if n % 2 else even_sum[:], conv_pad[:, p, j:j + T], dw[:, i, p, j:j + 1]
                                if n >= 2:
                                    dve.wait_ge(tap_done, n_dve * p + n - 1 + 2 * n_dve * i)
                                if n >= 2 or (n == 0 and later):
                                    if n == 0:
                                        dve.wait_ge(neg_c_ready, 1)
                                    ins = dve.scalar_tensor_tensor(out=dst, in0=src, scalar=w, in1=dst if n else neg_c[:],
                                                                   op0=ALU.mult, op1=ALU.add)
                                else:
                                    ins = dve.tensor_scalar(dst, src, w, None, ALU.mult)
                                ins.then_inc(tap_done, 1)
                    body(0, FIRST_BANKS)
                    with pairs(dve, 1, n_pairs) as i:
                        body(i, IN_BANKS)
                    put_together(cy[:, n_pairs - 1, 1, :], 1, ph.steps - 1, 0)
                    add_pool_sum(cy[:, n_pairs - 1, 1, :], 1, ph.steps - 1, 0)

                    dve.wait_ge(ln_part, 1)
                    dve.tensor_scalar(stat_part[:], columns(LN_PART, 0, 2 * NC), 1.0, None, ALU.mult).then_inc(ln_part_read, 1)

                    def centre(k):
                        dve.scalar_tensor_tensor(out=conv_y[:, k, :], in0=bank[LN_SUM][:], scalar=-1.0 / D_MODEL,
                                                 in1=conv_y[:, k, :], op0=ALU.mult, op1=ALU.add).then_inc(centred, 1)
                    dve.wait_ge(ln_part_read, 1)
                    dve.wait_ge(ln_stat, 1)
                    dve.tensor_tensor(stat[:], columns(LN_STAT, 0, 2 * NC), stat_part[:], ALU.add).then_inc(ln_step, 1)
                    dve.wait_ge(ln_step, 1)
                    dve.scalar_tensor_tensor(out=stat_part[:, 0:NC], in0=stat[:, 0:NC], scalar=-1.0 / D_MODEL,
                                             in1=stat[:, 0:NC], op0=ALU.mult, op1=ALU.mult).then_inc(ln_step, 1)
                    dve.wait_ge(ln_step, 2)
                    dve.tensor_tensor(stat[:, 0:NC], stat[:, NC:2 * NC], stat_part[:, 0:NC], ALU.add).then_inc(ln_step, 1)
                    dve.wait_ge(ln_root, 1)
                    dve.reciprocal(inv[:], root[:]).then_inc(ln_inv, 1)
                    dve.wait_ge(ln_inv, 1)
                    diagonal(ln_diag)
                    dve.wait_ge(ln_sum, 1)
                    for k in range(3):
                        centre(k)
                    dve.wait_ge(ln_cast, 1)
                    for k in range(KT + 1):
                        if k < KT:
                            dve.wait_ge(centred, k + 1)
                            dve.tensor_tensor(conv_y[:, k, :], conv_y[:, k, :], bank[LN_CAST][:],
                                              ALU.mult).then_inc(conv_scaled, 1)
                        if k + 3 < KT:
                            centre(k + 3)
                        if k >= 1:
                            dve.wait_ge(prod_hi, ph.prod0 + k)
                            dve.tensor_tensor(conv_lo[:, k - 1, :], conv_y[:, k - 1, :],
                                              conv_hi[:, k - 1, :].bitcast(F32), ALU.subtract).then_inc(prod_lo, 1)

                elif kind == "conv_out":
                    n = post_norm(q)
                    clear_acc(n)
                    for t in range(ph.steps):
                        for d in range(2):
                            if 2 * t + d < KT - 1:
                                add_sq(n, 2 * t + d, 0, d)
                        if t < ph.steps - 1:
                            split_lo(s0 + 2 + t, 0, 0, t % 2, ph.cols if t + 2 < ph.steps else ph.next_cols)

                if kind in ("ffn_out", "sgu_out", "conv_out"):
                    mean_square(post_norm(q), 0, slice(0, NC // 2))
                    inverse(post_norm(q), 0, slice(0, NC // 2))
                    if q + 1 < n_sub:
                        residual_and_prepare(q, q + 1, s0 + ph.steps)
                    else:
                        last_residual(q)

        @block.tensor
        def _(pe):
            def product(dst, slot, col, x_h, x_l, start, stop):
                w_h, w_l = w_hi[:, slot, col:col + P], w_lo[:, slot, col:col + P]
                pe.matmul(dst, w_h, x_h, start=start, stop=False)
                pe.matmul(dst, w_h, x_l, start=False, stop=False)
                return pe.matmul(dst, w_l, x_h, start=False, stop=stop)

            def column_sums(b, cs, parts, signal, at=0):
                for c in cs:
                    for j, part in enumerate(parts):
                        ins = pe.matmul(bank[b][:, at + c:at + c + 1], part[:, c * P:(c + 1) * P], ones[:, 0:1],
                                        start=(j == 0), stop=(j == len(parts) - 1))
                if signal:
                    ins.then_inc(signal, 1)

            def sum_of_acc(n):
                pe.wait_ge(acc_done, acc_base(n + 1))
                column_sums(CAST, range(NC), (acc[:],), stat_part_ready)

            def sum_of_last(n, h=0, cs=range(NC)):
                pe.wait_ge(sq_ready, sq_base(n + 1) - (cs.stop < NC))
                column_sums(STAT, cs, (sq[:, 1, :],), stat_ready)

            def broadcast(b, signal, half=slice(0, T)):
                pe.matmul(bank[b][:, half], ones[:], diag[:].rearrange("p c n -> p (c n)")[:, half], start=True,
                          stop=True).then_inc(signal, 1)

            def broadcast_half(n, h):
                pe.wait_ge(diag_ready, trip(n, h) + 1)
                broadcast(CAST_HALVES[h], cast_ready, HALVES[h])

            def last_half_product(q, h, slot, col, x_h, x_l, k, first, last, count):
                half, n = HALVES[h], post_norm(q)
                ins = product(bank[LAST_BANKS[h]][:, half], slot, col, x_h[:, half], x_l[:, half], first, last)
                if last:
                    ins.then_inc(step_used if h else last_half, 1)
                if h and k == SUM_AT:
                    sum_of_last(n, 0, range(NC // 2))
                if h and k == min(CAST_AT, count - 1):
                    broadcast_half(n, 0)
                return ins

            def second_sum(q):
                sum_of_last(post_norm(q), 1, range(NC // 2, NC))

            def first_steps(ph):
                q, n, s0 = ph.sub, pre_norm(ph.sub), ph.s0
                if q:
                    second_sum(q - 1)
                if q:
                    pe.wait_ge(split_done, s0 + 1)
                spots = [(t, j, bank[FIRST_BANKS[t][j]]) for t in range(2) for j in range(2)]
                for h, half in enumerate(HALVES):
                    for k in range(KT):
                        if q and h == 0 and k == 3:
                            broadcast_half(post_norm(q - 1), 1)
                        pe.wait_ge(xhi_ready, 2 * KT * q + KT * h + k + 1)
                        if q == 0 and h == 0 and k % 2 == 0:
                            if k // 2 < PIECES - 1:
                                pe.wait_ge(first_lo, k // 2 + 1)
                            else:
                                pe.wait_ge(split_done, 1)
                        for t, j, dst in spots:
                            if h == 0 and k % 2 == 0 and (t, j) == (1, 0):
                                if k // 2 < PIECES - 1:
                                    pe.wait_ge(lo_piece, 3 * (PIECES - 1) * q + k // 2 + 1)
                                else:
                                    pe.wait_ge(split_done, s0 + 2)
                            col = (2 * k + j) * P
                            pe.matmul(dst[:, half], w_hi[:, t, col:col + P], xn_hi[:, k, half], start=(k == 0), stop=False)
                            pe.matmul(dst[:, half], w_lo[:, t, col:col + P], xn_hi[:, k, half], start=False, stop=False)
                        if h and k == KT - 1:
                            sum_of_acc(n)
                            sum_of_last(n)
                        pe.wait_ge(xlo_ready, 2 * KT * q + KT * h + k + 1)
                        for t, j, dst in spots:
                            col = (2 * k + j) * P
                            ins = pe.matmul(dst[:, half], w_hi[:, t, col:col + P], xn_lo[:, k, half], start=False,
                                            stop=(k == KT - 1))
                            if h and k == KT - 1:
                                ins.then_inc(step_used if j else proj_ready, 1)
                        if h and k % 2 and k < KT - 1:
                            ins.then_inc(cols_used, 1)

            def third_step_first_tile(ph):
                for k in range(KT):
                    if k % 2 == 0 and k // 2 < PIECES - 1:
                        pe.wait_ge(lo_piece, 3 * (PIECES - 1) * ph.sub + PIECES - 1 + k + 1)
                    elif k % 2 == 0:
                        pe.wait_ge(split_done, ph.s0 + 3)
                    ins = product(bank[IN_BANKS[0][0]][:], 0, 2 * k * P, xn_hi[:, k, :], xn_lo[:, k, :],
                                  k == 0, k == KT - 1)
                    if k == BROADCAST_AT:
                        pe.wait_ge(diag_ready, trip(pre_norm(ph.sub)) + 1)
                        broadcast(CAST, cast_ready)
                ins.then_inc(proj_ready, 1)

            def in_tile(p, j):
                for k in range(KT):
                    ins = product(bank[IN_BANKS[p][j]][:], p, (2 * k + j) * P, xn_hi[:, k, :], xn_lo[:, k, :],
                                  k == 0, k == KT - 1)
                ins.then_inc(step_used if j else proj_ready, 1)

            pe.wait_ge(const_ready, 4)
            for ph in phases:
                s0, n_pairs, kind, q = ph.s0, ph.steps // 2, ph.kind, ph.sub
                if kind in ("ffn_in", "v", "conv_in"):
                    first_steps(ph)

                def begin(i, p, second_pair):
                    if second_pair and p == 0:
                        third_step_first_tile(ph)
                        return
                    pe.wait_ge(split_done, s0 + p + 1 + 2 * i)
                    pe.wait_ge(scaled, 2 * ph.in0 + 2 * p - 2 + 4 * i)
                    in_tile(p, 0)

                def in_pair(i, second_pair):
                    for p in range(2):
                        begin(i, p, second_pair)
                        in_tile(p, 1)

                if kind == "ffn_in":
                    in_pair(1, True)
                    with pairs(pe, 2, n_pairs) as i:
                        in_pair(i, False)

                if kind == "conv_in":
                    def taps(i, p, t_static):
                        pe.wait_ge(diag_built, 2 * len(PE_TAPS) * (t_static + 1) + 4 * len(PE_TAPS) * i)
                        pe.wait_ge(pad_ready, t_static + 1 + 2 * i)
                        if t_static >= 2 or not isinstance(i, int):
                            pe.wait_ge(conv_part, 3 * (t_static - 1) + 6 * i)
                        for n, j in enumerate(PE_TAPS):
                            dst, x_h, x_l = bank[TAP_BANKS[p]][:], pad_hi[:, p, j:j + T], pad_lo[:, p, j:j + T]
                            pe.matmul(dst, tap_hi[:, p, n, :], x_h, start=(n == 0), stop=False)
                            pe.matmul(dst, tap_hi[:, p, n, :], x_l, start=False, stop=False)
                            ins = pe.matmul(dst, tap_lo[:, p, n, :], x_h, start=False, stop=(n == len(PE_TAPS) - 1))
                        ins.then_inc(pe_taps, 1)

                    def conv_pair(i, second_pair):
                        for p in range(2):
                            begin(i, p, second_pair)
                            if second_pair and p == 0:
                                taps(0, 0, 0)
                            elif second_pair:
                                pe.wait_ge(conv_part, 3)
                                pe.matmul(bank[TAP_BANKS[0]][:], ones[:], conv_y[:, 0, :], start=True,
                                          stop=True).then_inc(c_ready, 1)
                                taps(0, 1, 1)
                            else:
                                taps(i, 1 - p, p - 1)
                            in_tile(p, 1)
                            if second_pair and p:
                                taps(0, 0, 2)
                    conv_pair(1, True)
                    with pairs(pe, 2, n_pairs) as i:
                        conv_pair(i, False)
                    pe.wait_ge(scaled, 2 * ph.in0 + 2 * KT)
                    pe.wait_ge(conv_sq_free, 2 * KT - 2)
                    pe.matmul(bank[LN_SUM][:], ones[:], acc[:], start=True, stop=False)
                    taps(0, 1, KT - 1)
                    pe.wait_ge(conv_part, 3 * (KT - 1))
                    pe.matmul(bank[LN_SUM][:], ones[:], conv_y[:, KT - 2, :], start=False, stop=False)
                    pe.wait_ge(conv_sq, KT - 1)
                    column_sums(LN_PART, range(NC), (acc[:], conv_y[:, KT - 2, :]), None)
                    column_sums(LN_PART, range(NC), (sq_sum[:], sq[:, 0, :]), ln_part, at=NC)
                    pe.wait_ge(conv_part, 3 * KT)
                    column_sums(LN_STAT, range(NC), (conv_y[:, KT - 1, :],), None)
                    pe.wait_ge(conv_sq, KT)
                    column_sums(LN_STAT, range(NC), (sq[:, 1, :],), ln_stat, at=NC)
                    pe.matmul(bank[LN_SUM][:], ones[:], conv_y[:, KT - 1, :], start=False, stop=True).then_inc(ln_sum, 1)
                    pe.wait_ge(ln_diag, 1)
                    broadcast(LN_CAST, ln_cast)

                if kind == "ffn_out":
                    def body(i, last):
                        for d in range(1 if last else 2):
                            pe.wait_ge(out_bank_free, ph.out0 + d + 1 + 2 * i)
                            for half in range(2):
                                pe.wait_ge(split_done, s0 + 2 * d + half + 1 + 4 * i)
                                pe.wait_ge(prod_lo, ph.prod0 + FH * (half + 1))
                                for kk in range(FH):
                                    k = half * FH + kk
                                    ins = product(bank[OUT_BANKS[d]][:], half, kk * P, h_hi[:, k, :], h_lo[:, k, :],
                                                  k == 0, k == FT - 1)
                                ins.then_inc(step_used, 1)
                    with pairs(pe, 0, n_pairs // 2 - 1) as i:
                        body(i, False)
                    body(n_pairs // 2 - 1, True)
                    pe.wait_ge(out_bank_free, ph.out0 + KT)
                    for b in range(2):
                        pe.wait_ge(split_done, s0 + 2 * (KT - 1) + b + 1)
                        for h in range(2):
                            for kk in range(FH):
                                k = b * FH + kk
                                if b:
                                    ins = last_half_product(q, h, b, kk * P, h_hi[:, k, :], h_lo[:, k, :], kk,
                                                            False, kk == FH - 1, FH)
                                else:
                                    ins = product(bank[LAST_BANKS[h]][:, HALVES[h]], b, kk * P, h_hi[:, k, HALVES[h]],
                                                  h_lo[:, k, HALVES[h]], kk == 0, False)
                        if b == 0:
                            ins.then_inc(step_used, 1)
                            sum_of_acc(post_norm(q))

                if kind == "v":
                    def turn(i, p, t_static):
                        for j, buf in enumerate((first, second)):
                            pe.wait_ge(act_done, ph.act0 + 2 * t_static + j + 1 + 4 * i)
                            if not isinstance(i, int) or i or t_static:
                                pe.wait_ge(v_copied, 2 * t_static + j - 1 + 4 * i)
                            for c in range(NC):
                                ins = pe.transpose(bank[MIX_BANKS[j]][:, c * P:(c + 1) * P],
                                                   buf[:, p, c * P:(c + 1) * P], ident[:])
                            ins.then_inc(v_turned, 1)

                    def v_pair(i, second_pair):
                        for p in range(2):
                            begin(i, p, second_pair)
                            in_tile(p, 1)
                            if p:
                                turn(i, 0, 0)
                            elif second_pair:
                                turn(0, 0, 0)
                                turn(0, 1, 1)
                            else:
                                turn(i, 1, -1)
                    v_pair(1, True)
                    with pairs(pe, 2, n_pairs) as i:
                        v_pair(i, False)
                    pe.wait_ge(ws_ready, 1)
                    for j in range(2):
                        ins = pe.matmul(bank[OUT_BANKS[j]][:], ones[:],
                                        ws_raw[:, 4 * j:4 * j + 4, :].rearrange("p g t -> p (g t)"), start=True, stop=True)
                    ins.then_inc(rowsum_mm, 1)
                    turn(0, 1, 2 * n_pairs - 1)

                if kind == "u":
                    wsh = ws_hi[:].rearrange("p (i g) t -> p i g t", g=2)
                    wsl = ws_lo[:].rearrange("p (i g) t -> p i g t", g=2)
                    with pairs(pe, 0, n_pairs) as i:
                        for p in range(2):
                            pe.wait_ge(split_done, s0 + p + 1 + 2 * i)
                            pe.wait_ge(scaled, 2 * ph.in0 + 2 * p - 2 + 4 * i)
                            in_tile(p, 0)
                            in_tile(p, 1)
                            pe.wait_ge(vs_ready, p + 1 + 2 * i)
                            if p:
                                pe.wait_ge(mixed_ready, 2 * p + 4 * i)
                            else:
                                pe.wait_ge(prod_ready, ph.prod0 + 4 * i)
                            for j in range(GT):
                                for c in range(NC):
                                    dst = bank[MIX_BANKS[j]][:, c * CHUNK:(c + 1) * CHUNK]
                                    v_h, v_l = vs_hi[:, c, j * P:(j + 1) * P], vs_lo[:, c, j * P:(j + 1) * P]
                                    pe.matmul(dst, v_h, wsh[:, i, p, :], start=True, stop=False)
                                    pe.matmul(dst, v_h, wsl[:, i, p, :], start=False, stop=False)
                                    ins = pe.matmul(dst, v_l, wsh[:, i, p, :], start=False, stop=True)
                            ins.then_inc(mix_ready, 1)

                if kind == "sgu_out":
                    def body(i, last):
                        for d in range(1 if last else 2):
                            pe.wait_ge(out_bank_free, ph.out0 + d + 1 + 2 * i)
                            pe.wait_ge(split_done, s0 + d + 1 + 2 * i)
                            for k in range(ST):
                                if k in (0, ST - 4, ST - 2):
                                    pe.wait_ge(prod_lo, ph.prod0 + (ST - 4 if k == 0 else k + 2))
                                ins = product(bank[OUT_BANKS[d]][:], d, k * P, gated[:, k // GT, 0, k % GT, :],
                                              gated[:, k // GT, 1, k % GT, :], k == 0, k == ST - 1)
                            ins.then_inc(step_used, 1)
                    with pairs(pe, 0, n_pairs - 1) as i:
                        body(i, False)
                    body(n_pairs - 1, True)
                    pe.wait_ge(out_bank_free, ph.out0 + KT)
                    pe.wait_ge(split_done, s0 + KT)
                    for h in range(2):
                        for k in range(ST):
                            ins = last_half_product(q, h, 1, k * P, gated[:, k // GT, 0, k % GT, :],
                                                    gated[:, k // GT, 1, k % GT, :], k, k == 0, k == ST - 1, ST)
                            if h == 0 and k == ST // 2:
                                sum_of_acc(post_norm(q))

                if kind == "conv_out":
                    def out_product(d, k):
                        ins = product(bank[CONV_OUT_BANKS[d]][:], d // 2 % 2, (d % 2 * KT + k) * P, conv_hi[:, k, :],
                                      conv_lo[:, k, :], k == 0, k == KT - 1)
                        if k == KT - 1:
                            ins.then_inc(step_used if d % 2 else half_step, 1)
                    pe.wait_ge(split_done, s0 + 2)
                    for k in range(KT):
                        pe.wait_ge(prod_lo, ph.prod0 + k + 1)
                        for d in range(3):
                            out_product(d, k)
                    for d in range(3, KT - 1):
                        pe.wait_ge(split_done, s0 + d // 2 + 1)
                        for k in range(KT):
                            out_product(d, k)
                    pe.wait_ge(out_bank_free, ph.out0 + KT - 1)
                    for h in range(2):
                        for k in range(KT):
                            ins = last_half_product(q, h, 1, (KT + k) * P, conv_hi[:, k, :], conv_lo[:, k, :], k,
                                                    k == 0, k == KT - 1, KT)
                            if h == 0 and k == KT // 2:
                                sum_of_acc(post_norm(q))

                if kind in ("ffn_out", "sgu_out", "conv_out") and q + 1 == n_sub:
                    second_sum(q)
                    broadcast_half(post_norm(q), 1)


def kernel(x, norm_g, ff_w_gate, ff_w_up, ff_w_down, sgu_w_in, sgu_ln_g, sgu_ln_b, sgu_w_spatial, sgu_b_spatial,
           sgu_w_out, conv_w_pw1, conv_w_dw, conv_b_dw, conv_ln_g, conv_ln_b, conv_w_pw2, _n_sub=len(SUBLAYERS)):
    import concourse.bacc as bacc
    from concourse.bass_utils import run_bass_kernel_spmd

    f = lambda a: np.asarray(a)
    feature = lambda a, tiles: f(a).reshape(tiles, P).T

    def in_blocks(parts, pairs_of_tiles):
        tiled = [f(w).reshape(KT, P, -1, P) for w in parts]
        return np.stack([np.stack([tiled[w][:, :, t, :] for w, t in step], axis=1).transpose(2, 0, 1, 3).reshape(P, BLOCK)
                         for step in pairs_of_tiles])

    gate, up = f(ff_w_gate).reshape(4, D_MODEL, D_FF), f(ff_w_up).reshape(4, D_MODEL, D_FF)
    down = f(ff_w_down).reshape(4, 2, FH, P, KT, P)
    arrays = {
        "x_in": f(x).reshape(T, KT, P).transpose(2, 1, 0),
        "params": np.concatenate(
            [f(norm_g).reshape(N_NORMS, KT, P).transpose(2, 0, 1).reshape(P, N_NORMS * KT),
             feature(sgu_ln_g, ST), feature(sgu_ln_b, ST), feature(conv_b_dw, KT), feature(conv_ln_g, KT),
             feature(conv_ln_b, KT),
             f(conv_w_dw).reshape(TAPS, KT, P).transpose(2, 1, 0).reshape(P, KT * TAPS)], axis=1),
        "sgu_spatial": f(sgu_w_spatial).reshape(GROUPS, CHUNK, CHUNK).transpose(2, 0, 1),
        "sgu_bias": f(sgu_b_spatial).reshape(GROUPS, CHUNK),
        "ffn_in_w": np.stack([in_blocks((gate[q], up[q]), [((0, t), (1, t)) for t in range(FT)]) for q in range(4)]),
        "ffn_out_w": down.transpose(0, 4, 1, 3, 2, 5).reshape(4, 2 * KT, P, DOWN),
        "sgu_in_w": in_blocks((f(sgu_w_in)[0],), [((0, ST + 2 * g), (0, ST + 2 * g + 1)) for g in range(GROUPS)]
                              + [((0, 2 * g), (0, 2 * g + 1)) for g in range(GROUPS)]),
        "sgu_out_w": f(sgu_w_out)[0].reshape(ST, P, KT, P).transpose(2, 1, 0, 3).reshape(KT, P, ST * P),
        "conv_in_w": in_blocks((f(conv_w_pw1)[0],), [((0, KT + t), (0, t)) for t in range(KT)]),
        "conv_out_w": f(conv_w_pw2)[0].reshape(KT, P, KT // 2, 2, P).transpose(2, 1, 3, 0, 4).reshape(KT // 2, P, BLOCK),
    }
    nc = bacc.Bacc("TRN2", target_bir_lowering=False, num_devices=1)
    arrays = {name: np.ascontiguousarray(a) for name, a in arrays.items()}
    args = {name: nc.dram_tensor(name, a.shape, mybir.dt.from_np(a.dtype), kind="ExternalInput").ap()
            for name, a in arrays.items()}
    out = nc.dram_tensor("out", (P, KT, T), F32, kind="ExternalOutput").ap()
    build_trunk(nc, out=out, n_sub=_n_sub, **args)
    r = run_bass_kernel_spmd(nc, [arrays], core_ids=[0])
    return np.ascontiguousarray(np.asarray(r.results[0]["out"]).transpose(2, 1, 0)).reshape(1, T, D_MODEL)
```
